# Optimizing a Trainium2 kernel written in Bass

```python
import jax
import jax.numpy as jnp
from jax import lax
import numpy as np

D_MODEL = 1024
BATCH = 1
SEQ = 1024
DEPTH = 2

HEAD_DIM = 64
N_MIX_HEADS = D_MODEL // HEAD_DIM
HEADS_A = (3 * N_MIX_HEADS) // 8
HEADS_B = (3 * N_MIX_HEADS) // 8
HEADS_C = N_MIX_HEADS - HEADS_A - HEADS_B
Q_LORA = D_MODEL // 4
KV_LORA = D_MODEL // 8
QK_NOPE = HEAD_DIM
QK_ROPE = HEAD_DIM // 2
V_DIM_A = HEAD_DIM
DILATED_PAIRS = ((128, 1), (512, 4), (2048, 16))
GRID_W = 64
NA_ROWS = 8
NA_COLS = 16
NA_QCOLS = 16
NA_KCOLS = 2 * NA_COLS
D_FF = 4 * D_MODEL
ROPE_THETA = 10000.0
Q_BLOCK = 128
NORM_EPS = 1e-6
NEG_INF = -1e30

COLS_A = Q_LORA + KV_LORA + QK_ROPE
COLS_B = 3 * HEADS_B * HEAD_DIM
COLS_C = 3 * HEADS_C * HEAD_DIM
IN_COLS = COLS_A + COLS_B + COLS_C
WIDTH_A = HEADS_A * V_DIM_A
WIDTH_B = HEADS_B * HEAD_DIM
WIDTH_C = HEADS_C * HEAD_DIM
MIX_WIDTH = WIDTH_A + WIDTH_B + WIDTH_C

kernel_name = "hybrid_mla_dilated_natten_encoder"

def rms_norm(x, g):
    xf = x.astype(jnp.float32)
    y = xf * lax.rsqrt(jnp.mean(xf * xf, axis=-1, keepdims=True) + NORM_EPS)
    return (y * g.astype(jnp.float32)).astype(x.dtype)

def rope(x, pos):
    half = x.shape[-1] // 2
    inv_freq = ROPE_THETA ** (-jnp.arange(half, dtype=jnp.float32) / half)
    ang = pos[:, None] * inv_freq[None, :]
    cos = jnp.cos(ang)[None, :, None, :]
    sin = jnp.sin(ang)[None, :, None, :]
    x1 = x[..., :half].astype(jnp.float32)
    x2 = x[..., half:].astype(jnp.float32)
    return jnp.concatenate([x1 * cos - x2 * sin, x1 * sin + x2 * cos], axis=-1).astype(x.dtype)

def dense_attention(q, k, v):
    b, s, h, dq = q.shape
    scale = dq ** -0.5
    qb = q.reshape(b, s // Q_BLOCK, Q_BLOCK, h, dq).transpose(1, 0, 2, 3, 4)

    def one_block(q_blk):
        sc = jnp.einsum('bqhd,bkhd->bhqk', q_blk, k, preferred_element_type=jnp.float32) * scale
        p = jax.nn.softmax(sc, axis=-1)
        return jnp.einsum('bhqk,bkhd->bqhd', p.astype(v.dtype), v)

    o = lax.map(one_block, qb)
    return o.transpose(1, 0, 2, 3, 4).reshape(b, s, h, v.shape[-1])

def banded_attention(q, k, v, half):
    bq, n, h, d = q.shape
    blk = half
    nb = -(-n // blk)
    n_pad = nb * blk
    qp = jnp.pad(q, ((0, 0), (0, n_pad - n), (0, 0), (0, 0))).reshape(bq, nb, blk, h, d)
    pad_kv = ((0, 0), (blk, n_pad - n + blk), (0, 0), (0, 0))
    kp = jnp.pad(k, pad_kv).reshape(bq, nb + 2, blk, h, d)
    vp = jnp.pad(v, pad_kv).reshape(bq, nb + 2, blk, h, d)
    kw = jnp.concatenate([kp[:, :-2], kp[:, 1:-1], kp[:, 2:]], axis=2)
    vw = jnp.concatenate([vp[:, :-2], vp[:, 1:-1], vp[:, 2:]], axis=2)
    q_idx = jnp.arange(n_pad).reshape(nb, blk)
    k_idx = jnp.arange(nb)[:, None] * blk - blk + jnp.arange(3 * blk)[None, :]
    mask = ((jnp.abs(q_idx[:, :, None] - k_idx[:, None, :]) <= half)
            & (k_idx[:, None, :] >= 0) & (k_idx[:, None, :] < n))
    sc = jnp.einsum('bnqhd,bnkhd->bnhqk', qp, kw, preferred_element_type=jnp.float32) * (d ** -0.5)
    sc = jnp.where(mask[None, :, None], sc, NEG_INF)
    m = jnp.max(sc, axis=-1, keepdims=True)
    p = jnp.exp(sc - m)
    den = jnp.sum(p, axis=-1)
    o = jnp.einsum('bnhqk,bnkhd->bnqhd', p.astype(v.dtype), vw).astype(jnp.float32)
    o = o / den.transpose(0, 1, 3, 2)[..., None]
    lse = (m[..., 0] + jnp.log(den)).transpose(0, 1, 3, 2)
    o = o.reshape(bq, n_pad, h, d)[:, :n]
    lse = lse.reshape(bq, n_pad, h)[:, :n]
    return o, lse

def dilated_sliding_attention(q, k, v):
    b, s, h, d = q.shape
    outs, lses = [], []
    for window, dil in DILATED_PAIRS:
        n = s // dil
        qc = q.reshape(b, n, dil, h, d).transpose(0, 2, 1, 3, 4).reshape(b * dil, n, h, d)
        kc = k.reshape(b, n, dil, h, d).transpose(0, 2, 1, 3, 4).reshape(b * dil, n, h, d)
        vc = v.reshape(b, n, dil, h, d).transpose(0, 2, 1, 3, 4).reshape(b * dil, n, h, d)
        o, lse = banded_attention(qc, kc, vc, window // (2 * dil))
        outs.append(o.reshape(b, dil, n, h, d).transpose(0, 2, 1, 3, 4).reshape(b, s, h, d))
        lses.append(lse.reshape(b, dil, n, h).transpose(0, 2, 1, 3).reshape(b, s, h))
    w = jax.nn.softmax(jnp.stack(lses, axis=-1), axis=-1)
    o = jnp.sum(jnp.stack(outs, axis=-1) * w[:, :, :, None, :], axis=-1)
    return o.astype(q.dtype)

def neighbourhood_attention(q, k, v, rpb):
    b, s, h, d = q.shape
    rows = s // GRID_W
    kr_win = min(NA_ROWS, rows)
    q_rows = kr_win
    k_rows = min(2 * kr_win, rows)
    nrb = -(-rows // q_rows)
    rows_pad = nrb * q_rows
    ncb = GRID_W // NA_QCOLS
    qg = jnp.pad(q.reshape(b, rows, GRID_W, h, d), ((0, 0), (0, rows_pad - rows), (0, 0), (0, 0), (0, 0)))
    qg = qg.reshape(b, nrb, q_rows, ncb, NA_QCOLS, h, d).transpose(0, 1, 3, 2, 4, 5, 6)
    r_q = jnp.arange(rows_pad).reshape(nrb, q_rows)
    r_start = jnp.clip(r_q - kr_win // 2, 0, rows - kr_win)
    c_q = jnp.arange(GRID_W).reshape(ncb, NA_QCOLS)
    c_start = jnp.clip(c_q - NA_COLS // 2, 0, GRID_W - NA_COLS)
    kr_idx = (jnp.clip(jnp.arange(nrb) * q_rows - kr_win // 2, 0, rows - k_rows)[:, None]
              + jnp.arange(k_rows)[None, :])
    kc_idx = (jnp.clip(jnp.arange(ncb) * NA_QCOLS - NA_COLS // 2, 0, GRID_W - NA_KCOLS)[:, None]
              + jnp.arange(NA_KCOLS)[None, :])
    kgrid = k.reshape(b, rows, GRID_W, h, d)
    vgrid = v.reshape(b, rows, GRID_W, h, d)
    ri = kr_idx[:, None, :, None]
    ci = kc_idx[None, :, None, :]
    kg = kgrid[:, ri, ci]
    vg = vgrid[:, ri, ci]
    row_ok = (kr_idx[:, None, :] >= r_start[:, :, None]) & (kr_idx[:, None, :] < r_start[:, :, None] + kr_win)
    col_ok = (kc_idx[:, None, :] >= c_start[:, :, None]) & (kc_idx[:, None, :] < c_start[:, :, None] + NA_COLS)
    dr = jnp.clip(kr_idx[:, None, :] - r_q[:, :, None], -(NA_ROWS - 1), NA_ROWS - 1) + (NA_ROWS - 1)
    dc = jnp.clip(kc_idx[:, None, :] - c_q[:, :, None], -(NA_COLS - 1), NA_COLS - 1) + (NA_COLS - 1)
    bias = rpb[:, dr[:, None, :, None, :, None], dc[None, :, None, :, None, :]]
    mask = row_ok[:, None, :, None, :, None] & col_ok[None, :, None, :, None, :]
    sc = jnp.einsum('bnmiphd,bnmjqhd->bnmhipjq', qg, kg, preferred_element_type=jnp.float32) * (d ** -0.5)
    sc = sc + bias.transpose(1, 2, 0, 3, 4, 5, 6).astype(jnp.float32)[None]
    sc = jnp.where(mask[:, :, None][None], sc, NEG_INF)
    shp = sc.shape
    p = jax.nn.softmax(sc.reshape(shp[:-2] + (k_rows * NA_KCOLS,)), axis=-1).reshape(shp)
    o = jnp.einsum('bnmhipjq,bnmjqhd->bnmiphd', p.astype(v.dtype), vg)
    o = o.transpose(0, 1, 3, 2, 4, 5, 6).reshape(b, rows_pad, GRID_W, h, d)[:, :rows]
    return o.reshape(b, s, h, d)

def setup_inputs(seed: int = 0) -> dict:
    key = jax.random.key(seed)
    ks = jax.random.split(key, 16)

    def normal(k, shape, scale):
        return jax.random.normal(k, shape, dtype=jnp.float32) * scale

    def gain(k, shape):
        return 1.0 + 0.02 * jax.random.normal(k, shape, dtype=jnp.float32)

    return {
        "x": normal(ks[0], (BATCH, SEQ, D_MODEL), 1.0),
        "g_mix": gain(ks[1], (DEPTH, D_MODEL)),
        "w_in": normal(ks[2], (DEPTH, D_MODEL, IN_COLS), D_MODEL ** -0.5),
        "q_norm": gain(ks[3], (DEPTH, Q_LORA)),
        "w_uq": normal(ks[4], (DEPTH, Q_LORA, HEADS_A * (QK_NOPE + QK_ROPE)), Q_LORA ** -0.5),
        "kv_norm": gain(ks[5], (DEPTH, KV_LORA)),
        "w_ukv": normal(ks[6], (DEPTH, KV_LORA, HEADS_A * (QK_NOPE + V_DIM_A)), KV_LORA ** -0.5),
        "rpb": normal(ks[7], (DEPTH, HEADS_C, 2 * NA_ROWS - 1, 2 * NA_COLS - 1), 0.1),
        "out_norm_a": gain(ks[8], (DEPTH, WIDTH_A)),
        "out_norm_b": gain(ks[9], (DEPTH, WIDTH_B)),
        "out_norm_c": gain(ks[10], (DEPTH, WIDTH_C)),
        "w_out": normal(ks[11], (DEPTH, MIX_WIDTH, D_MODEL), MIX_WIDTH ** -0.5),
        "g_mlp": gain(ks[12], (DEPTH, D_MODEL)),
        "w_mlp_in": normal(ks[13], (DEPTH, D_MODEL, D_FF), D_MODEL ** -0.5),
        "w_mlp_out": normal(ks[14], (DEPTH, D_FF, D_MODEL), D_FF ** -0.5),
        "g_final": gain(ks[15], (D_MODEL,)),
    }

def reference(x, g_mix, w_in, q_norm, w_uq, kv_norm, w_ukv, rpb, out_norm_a, out_norm_b, out_norm_c,
              w_out, g_mlp, w_mlp_in, w_mlp_out, g_final):
    b, s, _ = x.shape
    pos = jnp.arange(s, dtype=jnp.float32)
    for l in range(DEPTH):
        h = rms_norm(x, g_mix[l])
        proj = h @ w_in[l]
        p_a = proj[..., :COLS_A]
        p_b = proj[..., COLS_A:COLS_A + COLS_B]
        p_c = proj[..., COLS_A + COLS_B:]
        c_q = p_a[..., :Q_LORA]
        c_kv = p_a[..., Q_LORA:Q_LORA + KV_LORA]
        k_pe = p_a[..., Q_LORA + KV_LORA:]
        qa = (rms_norm(c_q, q_norm[l]) @ w_uq[l]).reshape(b, s, HEADS_A, QK_NOPE + QK_ROPE)
        kva = (rms_norm(c_kv, kv_norm[l]) @ w_ukv[l]).reshape(b, s, HEADS_A, QK_NOPE + V_DIM_A)
        k_pe = jnp.broadcast_to(rope(k_pe[:, :, None, :], pos), (b, s, HEADS_A, QK_ROPE))
        qa = jnp.concatenate([qa[..., :QK_NOPE], rope(qa[..., QK_NOPE:], pos)], axis=-1)
        ka = jnp.concatenate([kva[..., :QK_NOPE], k_pe], axis=-1)
        o_a = dense_attention(qa, ka, kva[..., QK_NOPE:])
        pb = p_b.reshape(b, s, 3, HEADS_B, HEAD_DIM)
        o_b = dilated_sliding_attention(rope(pb[:, :, 0], pos), rope(pb[:, :, 1], pos), pb[:, :, 2])
        pc = p_c.reshape(b, s, 3, HEADS_C, HEAD_DIM)
        o_c = neighbourhood_attention(pc[:, :, 0], pc[:, :, 1], pc[:, :, 2], rpb[l])
        mixed = jnp.concatenate([
            rms_norm(o_a.reshape(b, s, WIDTH_A), out_norm_a[l]),
            rms_norm(o_b.reshape(b, s, WIDTH_B), out_norm_b[l]),
            rms_norm(o_c.reshape(b, s, WIDTH_C), out_norm_c[l]),
        ], axis=-1)
        x = x + mixed @ w_out[l]
        h2 = rms_norm(x, g_mlp[l])
        x = x + jnp.square(jax.nn.relu(h2 @ w_mlp_in[l])) @ w_mlp_out[l]
    return rms_norm(x, g_final)


_drawn_inputs = setup_inputs


def setup_inputs(seed=0):
    import zlib

    import numpy as np

    out = dict(_drawn_inputs(seed))
    spreads = {}
    factors = {'q_norm': 6.867,
     'kv_norm': 3.184,
     'out_norm_a': 5.173,
     'out_norm_b': 5.138,
     'out_norm_c': 5.828,
     'g_mlp': 3.05,
     'g_final': 2.871}
    for name, (base, spread) in spreads.items():
        noise = np.random.default_rng([zlib.crc32(name.encode()), seed]).standard_normal(out[name].shape)
        drawn = base * np.exp(spread * noise) if base else spread * noise
        out[name] = jnp.asarray(drawn.astype(out[name].dtype))
    for name, factor in factors.items():
        out[name] = (out[name] * factor).astype(out[name].dtype)
    return out
```

```python
import concourse.bass as bass
from concourse import mybir
from contextlib import ExitStack

P = 128
DEPTH = 2
SEQ = 1024
DM = 1024
DFF = 4096
HD = 64
HA, HB, HC = 6, 6, 4
NH = HA + HB + HC
QL, KVL, RA = 256, 128, 32
GRID_W = 64
ROWS = SEQ // GRID_W
EPS = 1e-6
NEG = -1e30

ST = SEQ // P
KT = DM // P
HI, LO = 0, 1

CA = QL + KVL + RA
WIDTH = {"a": CA, "bq": HB * HD, "up": None, "bk": HB * HD, "bv": HB * HD, "cqk": 2 * HC * HD, "cv": HC * HD,
         "o0": DM // 2, "o1": DM // 2}
JOBS = list(WIDTH)
NJ = len(JOBS)
UQ_N, UQ_R, UK_N, UV_N = HA * HD, HA * RA, HA * HD, HA * HD
UQ = UQ_N + UQ_R
UKV = UK_N + UV_N

ULEN = 2048
FG = 256
NG = DFF // FG
FT = FG // P
MLP0 = 2 * NJ
NU = MLP0 + 2 * NG


def up_unit(g):
    return MLP0 + (2 * g - 1 if g else 0)


def down_unit(g):
    return MLP0 + (2 * g + 2 if g < NG - 1 else 2 * NG - 1)


def unit_len(job, half):
    if job == "up":
        return (2 * UQ, UKV)[half]
    return KT // 2 * WIDTH[job]


F_AQ, F_AK = 0, UQ_N
F_BQ, F_BK = F_AK + UK_N, F_AK + UK_N + HB * HD
F_CQ = F_BK + HB * HD
F_CK = F_CQ + HC * HD
F_AR = F_CK + HC * HD
NF = F_AR + UQ_R + RA

CKR, CKC = 12, 32
CW = CKR * CKC


def c_cols(cb):
    return min(max(16 * cb - 8, 0), GRID_W - CKC)


def key_row0(half):
    return 4 * half


HEADS = [("A", h) for h in range(HA)] + [("B", HA + h) for h in range(HB)] + [("C", HA + HB + h) for h in range(HC)]
ITEMS = [(kind, h, i) for kind, h in HEADS for i in range(8)]
NI = len(ITEMS)
NB = NI // 4
GROUPS = []
ITEM_GROUPS = []
for n_, (kind_, _, _) in enumerate(ITEMS):
    ITEM_GROUPS.append([])
    for half_ in range(1 if kind_ == "C" else 2):
        ITEM_GROUPS[-1].append(len(GROUPS))
        GROUPS.append((n_, half_))
NGR = len(GROUPS)


def schedule():
    ev = []

    def split(job):
        return [("split", job, 0), ("split", job, 1)]

    for s in range(ST):
        ev.append(("acc", "a", s))
    for s in range(ST):
        ev.append(("acc", "bq", s))
        if s:
            ev.append(("turn", "bq", s - 1))
        if s == 1:
            ev += split("up")
        if s == ST - 2:
            ev.append(("turn", "lat", 0))
    for s in range(ST + 2):
        if s < ST:
            ev += [("acc", "uq", s), ("acc", "ur", s)]
        if s == 0:
            ev.append(("turn", "bq", ST - 1))
        if s >= 3:
            ev.append(("turn", "bk", s - 3))
        if 1 <= s <= ST:
            ev.append(("turn", "uk", s - 1))
        if s < ST - 1:
            ev.append(("turn", "lat", s + 1))
        if s >= 2:
            ev.append(("acc", "bk", s - 2))
        if s == ST:
            ev += split("bv")
        if s < ST:
            ev += [("turn", "uq", s), ("turn", "ur", s), ("acc", "uk", s), ("acc", "uv", s)]
        if s < 2:
            ev.append(("split", "bk", s))
    for s in range(ST):
        ev.append(("acc", "bv", s))
        if s == 0:
            ev.append(("turn", "bk", ST - 1))
        if s == 1:
            ev += split("cqk")
    for s in range(ST):
        ev.append(("acc", "cqk", s))
        if s:
            ev.append(("turn", "cqk", s - 1))
        if s == 1:
            ev += split("cv")
    for s in range(ST):
        ev.append(("acc", "cv", s))
        if s == 0:
            ev.append(("turn", "cqk", ST - 1))
    return ev


EVENTS = schedule()
JOB_OF = {"uq": "up", "ur": "up", "uk": "up", "uv": "up"}
OUT_TILES = [("acc", o, s) for o in ("o0", "o1") for s in range(ST)]
ACCS = [e for e in EVENTS if e[0] == "acc"] + OUT_TILES
ACT_FREES = ("a", "uq", "uk", "cqk")
TURNS = [e for e in EVENTS if e[0] == "turn"]


def job_end(job):
    return max(n for n, e in enumerate(ACCS) if JOB_OF.get(e[1], e[1]) == job) + 1


STAGED = [e for e in ACCS if e[1] in ("bq", "bk", "uq", "ur", "uk", "cqk")]
VSTAGED = [e for e in ACCS if e[1] in ("uv", "bv", "cv")]
NSTG = 4
NTB = 4
NTS = 3
TURN = {"bq": ([P] * 3, F_BQ), "bk": ([P] * 3, F_BK), "uq": ([P] * 3, F_AQ), "uk": ([P] * 3, F_AK),
        "ur": ([P, 96], F_AR), "cqk": ([P] * 4, F_CQ), "lat": ([P] * 3, None)}
STORED = [e for e in TURNS if e[1] != "lat"]


def frees_before(n, act):
    return sum((e[1] in ACT_FREES) == act for e in ACCS[:n])


ACT_FREE_N, DVE_FREE_N = frees_before(len(ACCS), True), frees_before(len(ACCS), False)


def encoder(nc, x_in, wstream, gains, lat_gains, cos_in, sin_in, bias_b, bias_c, ident_in, pair_in, g_final, out):
    f32, f32r = mybir.dt.float32, mybir.dt.float32r
    ALU, ACT, AX = mybir.AluOpType, mybir.ActivationFunctionType, mybir.AxisListType

    feats = nc.dram_tensor("feats", [2, NF, SEQ], f32).ap()
    values = nc.dram_tensor("values", [SEQ, NH * 2 * HD], f32).ap()
    x_park = nc.dram_tensor("x_park", [ST, P, DM], f32).ap()

    KB = 1024
    at = {}
    top = (nc.sbuf_base + 31) // 32 * 32
    for name, size in [("R0", 32 * KB), ("H", 64 * KB), ("WS", 64 * KB), ("RAW", 16 * KB), ("HN", 8 * KB),
                       ("LAT", 13312), ("ROPE", 2 * KB), ("ID", 512 + 256), ("GB", 4 * KB), ("GL", 1536),
                       ("STAT", 2304 + 64)]:
        at[name] = top
        top += size

    def sb(name, shape, dt, region, offset=0):
        return nc.alloc_sbuf_tensor_at(name, shape, dt, offset=at[region] + offset)

    x = sb("x", [P, ST, DM], f32, "R0")
    hT = sb("hT", [P, 2, KT, SEQ], f32r, "H")
    ws = [sb(f"ws{k}", [P, 2, 4096], f32r, "WS", k * 32 * KB) for k in range(2)]
    hid = sb("hid", [P, 2, 2, FT, SEQ], f32r, "WS")
    w_up = sb("w_up", [P, 2, KT, FG], f32r, "WS", 32 * KB)
    w_dn = sb("w_dn", [P, 2, FT, DM], f32r, "WS", 48 * KB)
    raw = sb("raw", [P, 2, ULEN], f32, "RAW")
    hn = sb("hn", [P, 2, DM], f32, "HN")
    lat = sb("lat", [P, ST, CA], f32, "LAT")
    cos = sb("cos", [P, ST, 32], f32, "ROPE")
    sin = sb("sin", [P, ST, 32], f32, "ROPE", KB)
    ident = sb("ident", [P, P], f32, "ID")
    pair = sb("pair", [P, HD], f32, "ID", 512)
    gB = sb("gB", [P, DM], f32, "GB")
    gL = sb("gL", [P, QL + KVL], f32, "GL")
    st_ss = sb("st_ss", [P, 4], f32, "STAT")
    st_sd = sb("st_sd", [P, 4], f32, "STAT", 32)
    st_rs = sb("st_rs", [P, 4], f32, "STAT", 64)
    sl_ss = sb("sl_ss", [P, 2, 2], f32, "STAT", 96)
    sl_sd = sb("sl_sd", [P, 2, 2], f32, "STAT", 128)
    sl_rs = sb("sl_rs", [P, 2, 2], f32, "STAT", 160)
    eps = sb("eps", [P, 1], f32, "STAT", 192)
    a_nm = sb("a_nm", [P, NI], f32, "STAT", 256 + 512)
    a_den = sb("a_den", [P, NI], f32, "STAT", 256 + 1024)
    a_rd = sb("a_rd", [P, NI], f32, "STAT", 256 + 1536)
    tst = sb("tst", [P, NTS, 2, 4, P], f32r, "R0")
    latT = sb("latT", [P, 2, 2, 3, P], f32r, "R0", 12 * KB)
    vst = sb("vst", [P, 2, 6, 2 * HD], f32r, "R0", 18 * KB)
    stage = sb("stage", [P, NSTG, 512], f32, "R0", 24 * KB)
    O = sb("O", [P, ST, DM], f32, "R0")
    head = [sb(f"head{k}", [P, 5 * 1024], f32r, "H", k * 20 * KB) for k in range(2)]
    kR = sb("kR", [P, SEQ], f32r, "H", 40 * KB)
    prob = sb("prob", [P, 2, 1024], f32, "H", 44 * KB)
    oT = sb("oT", [P, 1024], f32, "H", 52 * KB)
    biasC = [sb("biasC0", [P, 4, CW], f32, "HN"), sb("biasC1", [P, 4, CW], f32, "H", 56 * KB)]
    tabB = sb("tabB", [P, 1920], f32, "LAT")
    pT = sb("pT", [P, 2, 2, 8, 512], f32r, "WS")
    rbuf = sb("rbuf", [P, 2, 512], f32, "HN")
    vbuf = sb("vbuf", [P, 2, 512], f32, "HN", 4 * KB)

    ctx = ExitStack()
    with ctx:
        ps = ctx.enter_context(nc.psum_tensor("ps", [P, 8, 512], f32))

        def sem(name):
            return ctx.enter_context(nc.semaphore(name))

        const_in = sem("const_in")
        eps_set = sem("eps_set")
        x_loaded = sem("x_loaded")
        gain_in = sem("gain_in")
        gl_in = sem("gl_in")
        gain_free = sem("gain_free")
        raw_in = [sem(f"raw_in{k}") for k in range(2)]
        split_hi = sem("split_hi")
        split_lo = sem("split_lo")
        ss_ready, sd_ready, hn_ready = sem("ss_ready"), sem("sd_ready"), sem("hn_ready")
        nt_done, nt_hi, nt_free = sem("nt_done"), sem("nt_hi"), sem("nt_free")
        acc_done = sem("acc_done")
        acc_free_act, acc_free_dve = sem("acc_free_act"), sem("acc_free_dve")
        lat_sd, lat_ready = sem("lat_sd"), sem("lat_ready")
        turn_done, turn_hi, turn_lo = sem("turn_done"), sem("turn_hi"), sem("turn_lo")
        v_hi = sem("v_hi")
        tst_out = [sem(f"tst_out{k}") for k in range(NTS)]
        vst_out = [sem(f"vst_out{k}") for k in range(2)]
        parked = sem("parked")
        x_back = sem("x_back")
        stage_end = sem("stage_end")
        tab_in = sem("tab_in")
        head_in = [sem(f"head_in{k}") for k in range(2)]
        value_in = [sem(f"value_in{k}") for k in range(2)]
        biasc_neg = sem("biasc_neg")
        biasc_in = [sem(f"biasc_in{k}") for k in range(2)]
        s_done, mx_ready, p_ready, pn_ready = sem("s_done"), sem("mx_ready"), sem("p_ready"), sem("pn_ready")
        t_done, t_hi, t_lo = sem("t_done"), sem("t_hi"), sem("t_lo")
        pv_done, ot_ready, mg_done, o_ready = sem("pv_done"), sem("ot_ready"), sem("mg_done"), sem("o_ready")
        up_tile, relu_done, hid_ready = sem("up_tile"), sem("relu_done"), sem("hid_ready")
        down_tile, down_free = sem("down_tile"), sem("down_free")
        fin_ready = sem("fin_ready")
        fin_out = [sem(f"fin_out{k}") for k in range(2)]

        NBAR = 3
        TN = 3 * 2 * ST
        N_HN = 3 * ST

        def barrier(eng, l, k):
            if eng is nc.sync:
                eng.sem_inc(stage_end, 1)
            else:
                eng.drain().then_inc(stage_end, 1)
            eng.wait_ge(stage_end, (l * NBAR + k + 1) * 4)
            hold(eng)

        passed = sem("passed")

        def hold(eng):
            eng.sem_inc(passed, 1)

        def unit_of(job, half):
            return 2 * JOBS.index(job) + half

        def w_view(job, w):
            s = ws[JOBS.index(job) % 2]
            return s[:, w, 0:KT * WIDTH[job]].rearrange("p (k n) -> p k n", n=WIDTH[job])

        def up_views(kind, w):
            s = ws[JOBS.index("up") % 2]
            uq = s[:, w, 0:2 * UQ].rearrange("p (k n) -> p k n", n=UQ)
            ukv = s[:, w, 2 * UQ:2 * UQ + UKV]
            return {"uq": [(0, uq[:, 0, 0:UQ_N]), (1, uq[:, 1, 0:UQ_N])],
                    "ur": [(0, uq[:, 0, UQ_N:UQ]), (1, uq[:, 1, UQ_N:UQ])],
                    "uk": [(2, ukv[:, 0:UK_N])], "uv": [(2, ukv[:, UK_N:UKV])]}[kind]

        def width_of(kind):
            return {"uq": UQ_N, "ur": UQ_R, "uk": UK_N, "uv": UV_N}.get(kind) or WIDTH[kind]

        def words(ap):
            return ap.bitcast(f32)

        def from_grid(bank, j):
            return bank[:, j * P:(j + 1) * P].rearrange("p (r b c) -> p b r c", r=2, b=4)

        def by_block(ap):
            return ap.rearrange("p (b r c) -> p b r c", r=2, b=4)

        block = ctx.enter_context(nc.Block())

        @block.sync
        def _(sp):
            sp.dma_start(ident[:, :], ident_in).then_inc(const_in, 16)
            sp.dma_start(pair[:, :], pair_in).then_inc(const_in, 16)
            sp.dma_start(cos[:, :, :], cos_in).then_inc(const_in, 16)
            sp.dma_start(sin[:, :, :], sin_in).then_inc(const_in, 16)
            for t in range(ST):
                sp.dma_start(x[:, t, :], x_in[t * P:(t + 1) * P, :]).then_inc(x_loaded, 16)

            def load_unit(l, u, length=ULEN):
                sp.wait_ge(split_lo, l * NU + u + 1)
                hold(sp)
                sp.dma_start(raw[:, u % 2, 0:length], wstream[l, u, :, 0:length]).then_inc(raw_in[u % 2], 16)

            def load_gain(l, k):
                sp.wait_ge(gain_free, l * 3 + k + 1)
                hold(sp)
                sp.dma_start(gB[:, :], gains[l, k]).then_inc(gain_in, 16)

            with sp.Fori(0, DEPTH) as l:
                load_gain(l, 0)
                sp.dma_start(gL[:, :], lat_gains[l]).then_inc(gl_in, 16)
                for u in range(4):
                    load_unit(l, u, unit_len(JOBS[u // 2], u % 2))
                for t in range(ST):
                    sp.wait_ge(hn_ready, l * N_HN + t + 1)
                    sp.dma_start(x_park[t], x[:, t, :]).then_inc(parked, 16)
                load_gain(l, 1)
                for u in (4, 5):
                    load_unit(l, u, unit_len(JOBS[u // 2], u % 2))
                turn = vt = 0
                for e in EVENTS:
                    if e[0] == "split":
                        u = unit_of(e[1], e[2]) + 2
                        load_unit(l, u, unit_len(JOBS[u // 2], u % 2))
                    elif e in STORED:
                        n = TURNS.index(e)
                        k = turn % NTS
                        sp.wait_ge(turn_lo, l * len(TURNS) + n + 1)
                        cols = slice(e[2] * P, (e[2] + 1) * P)
                        widths, f0 = TURN[e[1]]
                        if e[1] == "ur":
                            for j, wd in enumerate(widths):
                                sp.dma_start(feats[:, f0 + j * P:f0 + j * P + wd, cols].rearrange("w p s -> p w s"),
                                             words(tst[0:wd, k, :, j, :])).then_inc(tst_out[k], 16)
                        elif e[1] == "cqk":
                            r = 2 * P // GRID_W * 8
                            for w in range(2):
                                for j in range(2):
                                    sp.dma_start(
                                        feats[w, F_CQ + j * P:F_CQ + (j + 1) * P, :]
                                        .rearrange("p (b s) -> p b s", b=4)[:, :, r * e[2]:r * (e[2] + 1)],
                                        words(tst[:, k, w, j, :]).rearrange("p (b s) -> p b s", b=4))\
                                      .then_inc(tst_out[k], 16)
                                sp.dma_start(
                                    feats[w, F_CK:F_CK + 2 * P, cols].rearrange("(j p) s -> p j s", p=P),
                                    words(tst[:, k, w, 2:4, :])).then_inc(tst_out[k], 16)
                        else:
                            nj = len(widths)
                            for w in range(2):
                                sp.dma_start(
                                    feats[w, f0:f0 + nj * P, cols].rearrange("(j p) s -> p j s", p=P),
                                    words(tst[:, k, w, 0:nj, :])).then_inc(tst_out[k], 16)
                        turn += 1
                    elif e in VSTAGED:
                        k = vt % 2
                        sp.wait_ge(acc_free_dve, l * DVE_FREE_N + frees_before(ACCS.index(e) + 1, False))
                        h0, nh = {"uv": (0, HA), "bv": (HA, HB), "cv": (HA + HB, HC)}[e[1]]
                        sp.dma_start(values[e[2] * P:(e[2] + 1) * P, h0 * P:(h0 + nh) * P],
                                     words(vst[:, k, 0:nh, :].rearrange("p h d -> p (h d)"))).then_inc(vst_out[k], 16)
                        vt += 1
                for k in range(NTS):
                    sp.wait_ge(tst_out[k], (l + 1) * 16 * TST_N[k])
                    hold(sp)
                for k in range(2):
                    sp.wait_ge(vst_out[k], (l + 1) * 16 * (len(VSTAGED) // 2))
                    hold(sp)
                sp.wait_ge(parked, (l + 1) * 16 * ST)
                hold(sp)
                barrier(sp, l, 0)

                sp.dma_start(tabB[:, :], bias_b).then_inc(tab_in, 16)
                for q, w in enumerate((HI, LO, HI, LO)):
                    sp.dma_start(words(kR[32 * q:32 * q + 32, :]), feats[w, F_AR + UQ_R:F_AR + UQ_R + RA, :])\
                      .then_inc(tab_in, 16)
                for n, (kind, h) in enumerate(HEADS):
                    k = n % 2
                    if n >= 2:
                        sp.wait_ge(s_done, l * NI + 8 * (n - 1))
                    hb = words(head[k][:, :])
                    kh = h if kind == "A" else h - HA if kind == "B" else h - HA - HB
                    fq = {"A": F_AQ, "B": F_BQ, "C": F_CQ}[kind] + kh * HD
                    fk = {"A": F_AK, "B": F_BK, "C": F_CK}[kind] + kh * HD
                    for part in range(2):
                        rows = slice(64 * part, 64 * part + 64)
                        sp.dma_start(hb[rows, 0:1024], feats[part, fq:fq + HD, :]).then_inc(head_in[k], 16)
                        for w in range(2):
                            sp.dma_start(hb[rows, 1024 * (1 + w):1024 * (2 + w)], feats[w, fk:fk + HD, :])\
                              .then_inc(head_in[k], 16)
                    if kind == "A":
                        for q, w in enumerate((HI, HI, LO, LO)):
                            sp.dma_start(hb[32 * q:32 * q + 32, 3072:4096],
                                         feats[w, F_AR + kh * RA:F_AR + (kh + 1) * RA, :]).then_inc(head_in[k], 16)

                    def load_bias(nc_half):
                        if nc_half >= 2:
                            sp.wait_ge(mx_ready, l * NI + 8 * (HA + HB) + 4 * (nc_half - 1))
                        sp.dma_start(biasC[nc_half % 2][:, :, :], bias_c[l, kh, nc_half % 2])\
                          .then_inc(biasc_in[nc_half % 2], 16)

                    if kind == "C":
                        load_bias(2 * kh)
                    if n >= 2:
                        sp.wait_ge(pv_done, l * NB + 2 * (n - 1))
                    if kind != "C":
                        sp.dma_start(hb[:, 4096:5120].rearrange("p (t d) -> p t d", d=P),
                                     values[:, h * P:(h + 1) * P].rearrange("(t p) d -> p t d", p=P))\
                          .then_inc(value_in[k], 16)
                    else:
                        grid = values.rearrange("(r c) d -> r c d", c=GRID_W)
                        for cb in range(4):
                            for rr in range(4):
                                dst = hb[32 * rr:32 * rr + 32, 3072 + 512 * cb:3072 + 512 * (cb + 1)]
                                src = grid[rr:rr + 13:4, c_cols(cb):c_cols(cb) + CKC, h * P:(h + 1) * P]
                                sp.dma_start(dst.rearrange("c (g d) -> c g d", d=P),
                                             src.rearrange("g c d -> c g d")).then_inc(value_in[k], 16)
                        load_bias(2 * kh + 1)
                barrier(sp, l, 1)

                for t in range(ST):
                    sp.wait_ge(hn_ready, l * N_HN + ST + t + 1)
                    sp.dma_start(x[:, t, :], x_park[t]).then_inc(x_back, 16)
                load_unit(l, 16)
                load_unit(l, 17)
                load_gain(l, 2)
                with sp.Fori(0, NG) as g:
                    load_unit_pair = l * NU + MLP0 + 2 * g
                    for k in range(2):
                        sp.wait_ge(split_lo, load_unit_pair + k + 1)
                        hold(sp)
                        sp.dma_start(raw[:, k, :], wstream[l, MLP0 + 2 * g + k]).then_inc(raw_in[k], 16)
                barrier(sp, l, 2)
            sp.wait_ge(gain_free, DEPTH * 3 + 1)
            sp.dma_start(gB[:, :], g_final).then_inc(gain_in, 16)
            for t in range(ST):
                sp.wait_ge(fin_ready, t + 1)
                sp.dma_start(out[t * P:(t + 1) * P, :], hn[:, t % 2, :]).then_inc(fin_out[t % 2], 16)
            for k in range(2):
                sp.wait_ge(fin_out[k], 16 * (ST // 2))

        @block.gpsimd
        def _(pool):
            pool.memset(eps[:, :], EPS).then_inc(eps_set, 1)

        @block.scalar
        def _(act):
            act.wait_ge(const_in, 16 * 4)
            act.wait_ge(eps_set, 1)

            def split_unit(l, u, dst):
                act.wait_ge(raw_in[u % 2], (l * (NU // 2) + u // 2 + 1) * 16)
                act.activation(dst, raw[:, u % 2, 0:dst.shape[-1]], ACT.Copy).then_inc(split_hi, 1)

            def split_job(l, job, half):
                j = JOBS.index(job)
                if 2 <= j < 7:
                    act.wait_ge(acc_done, l * len(ACCS) + job_end(JOBS[j - 2]))
                off = half * unit_len(job, 0)
                split_unit(l, unit_of(job, half), ws[j % 2][:, HI, off:off + unit_len(job, half)])

            def norm_stats(l, base, t, src, groups):
                if t or base:
                    act.wait_ge(hn_ready, l * N_HN + base + t)
                for k, (a, b) in enumerate(groups):
                    ins = act.activation(hn[:, t % 2, a:b], src[:, t, a:b], ACT.Square, scale=float(b - a) ** -0.5,
                                         accum_out=st_ss[:, k:k + 1])
                act.drain()
                act.activation(st_sd[:, 0:len(groups)], st_ss[:, 0:len(groups)], ACT.Sqrt, bias=eps[:, 0:1])\
                   .then_inc(sd_ready, 1)

            def norm_hi(l, base, t):
                for hf in range(2):
                    n = 2 * (base + t) + hf
                    act.wait_ge(nt_done, l * TN + n + 1)
                    act.activation(hT[:, HI, 4 * hf:4 * hf + 4, t * P:(t + 1) * P],
                                   ps[:, 6 + hf, :].rearrange("p (k s) -> p k s", s=P), ACT.Copy).then_inc(nt_hi, 1)

            def norm(l, base, src, groups, before):
                for t in range(ST + 1):
                    if t < ST:
                        before(t)
                        if t >= 2:
                            act.wait_ge(nt_done, l * TN + 2 * (base + t - 1))
                        norm_stats(l, base, t, src, groups)
                    if t:
                        norm_hi(l, base, t - 1)

            with act.Fori(0, DEPTH) as l:
                for hf in range(2):
                    split_job(l, "a", hf)
                norm(l, 0, x, [(0, DM)], lambda t: act.wait_ge(x_loaded, 16 * ST))
                for hf in range(2):
                    split_job(l, "bq", hf)
                acc = turn = stg = vt = st_turn = 0
                for e in EVENTS:
                    if e[0] == "split":
                        split_job(l, e[1], e[2])
                    elif e[0] == "acc":
                        kind, s = e[1], e[2]
                        bank = ps[:, acc % 4, :]
                        wd = width_of(kind)
                        if kind == "a":
                            act.wait_ge(acc_done, l * len(ACCS) + acc + 1)
                            act.activation(lat[:, s, :], bank[:, 0:CA], ACT.Copy)
                            act.drain()
                            if s >= 2:
                                act.wait_ge(lat_ready, l * ST + s - 1)
                            act.activation(bank[:, 0:QL], bank[:, 0:QL], ACT.Square, scale=float(QL) ** -0.5,
                                           accum_out=sl_ss[:, s % 2, 0:1])
                            act.activation(bank[:, QL:QL + KVL], bank[:, QL:QL + KVL], ACT.Square,
                                           scale=float(KVL) ** -0.5, accum_out=sl_ss[:, s % 2, 1:2])
                            act.drain().then_inc(acc_free_act, 1)
                            act.activation(sl_sd[:, s % 2, :], sl_ss[:, s % 2, :], ACT.Sqrt, bias=eps[:, 0:1])\
                               .then_inc(lat_sd, 1)
                        elif kind in ("uq", "uk", "cqk"):
                            act.wait_ge(acc_done, l * len(ACCS) + acc + 1)
                            if stg >= NSTG:
                                act.wait_ge(turn_done, l * len(TURNS) + turn_of(stg - NSTG) + 1)
                            dst = stage[:, stg % NSTG, :]
                            if kind == "cqk":
                                act.activation(dst[:, 0:wd // 2], bank[:, 0:wd // 2], ACT.Copy, scale=-HD ** -0.5)
                                act.activation(dst[:, wd // 2:wd], bank[:, wd // 2:wd], ACT.Copy)
                            else:
                                act.activation(dst[:, 0:wd], bank[:, 0:wd], ACT.Copy,
                                               scale=(HD + RA) ** -0.5 if kind == "uq" else 1.0)
                            act.drain().then_inc(acc_free_act, 1)
                        elif e in VSTAGED:
                            act.wait_ge(acc_done, l * len(ACCS) + acc + 1)
                            if vt >= 2:
                                act.wait_ge(vst_out[vt % 2], (l * (len(VSTAGED) // 2) + vt // 2) * 16)
                            elif vt == 0:
                                act.wait_ge(parked, (l + 1) * 16 * ST)
                            nh = wd // HD
                            act.activation(vst[:, vt % 2, 0:nh, 0:HD],
                                           bank[:, 0:wd].rearrange("p (h d) -> p h d", d=HD), ACT.Copy)\
                               .then_inc(v_hi, 1)
                            vt += 1
                        if e in STAGED:
                            stg += 1
                        acc += 1
                    else:
                        bank = ps[:, 4 + turn % NTB, :]
                        nj = len(TURN[e[1]][0])
                        act.wait_ge(turn_done, l * len(TURNS) + turn + 1)
                        if turn == 0:
                            act.wait_ge(parked, (l + 1) * 16 * ST)
                        if e[1] == "lat":
                            if e[2] >= 2:
                                act.wait_ge(acc_done, l * len(ACCS) + ACCS.index(("acc", "uv", e[2] - 2)) + 1)
                            act.activation(latT[:, e[2] % 2, HI, :, :],
                                           bank[:, 0:3 * P].rearrange("p (k s) -> p k s", s=P), ACT.Copy)\
                               .then_inc(turn_hi, 1)
                        else:
                            k = st_turn % NTS
                            if st_turn >= NTS:
                                act.wait_ge(tst_out[k], (l * TST_N[k] + TST_BEFORE[st_turn]) * 16)
                            if e[1] == "ur":
                                act.activation(tst[:, k, HI, 0, :], bank[:, 0:P], ACT.Copy)
                                act.activation(tst[0:96, k, HI, 1, :], bank[0:96, P:2 * P], ACT.Copy)
                                act.drain().then_inc(turn_hi, 1)
                            elif e[1] == "cqk":
                                for j in range(2):
                                    act.activation(by_block(tst[:, k, HI, j, :]), from_grid(bank, j), ACT.Copy)
                                act.activation(tst[:, k, HI, 2:4, :],
                                               bank[:, 2 * P:4 * P].rearrange("p (k s) -> p k s", s=P), ACT.Copy)
                                act.drain().then_inc(turn_hi, 1)
                            else:
                                act.activation(tst[:, k, HI, 0:nj, :],
                                               bank[:, 0:nj * P].rearrange("p (k s) -> p k s", s=P), ACT.Copy)\
                                   .then_inc(turn_hi, 1)
                            st_turn += 1
                        turn += 1
                barrier(act, l, 0)

                for i in range(NI + 8):
                    if 2 <= i < NI + 2:
                        it = i - 2
                        b = it // 4
                        if it % 4 == 0 and b >= 2:
                            act.wait_ge(pv_done, l * NB + b - 1)
                        for g in ITEM_GROUPS[it]:
                            act.wait_ge(t_done, l * NGR + g + 1)
                            nk, k0 = group_keys(g)
                            act.activation(pT[:, b % 2, HI, k0:k0 + nk, (it % 4) * P:(it % 4 + 1) * P],
                                           ps[:, 4 + g % 2, 0:nk * P].rearrange("p (k s) -> p k s", s=P), ACT.Copy)\
                               .then_inc(t_hi, 1)
                    if i < NI:
                        kind = ITEMS[i][0]
                        wd = CW if kind == "C" else SEQ
                        act.wait_ge(mx_ready, l * NI + i + 1)
                        if i >= 2:
                            act.wait_ge(t_done, l * NGR + ITEM_GROUPS[i - 2][-1] + 1)
                        s_in = ps[:, 2 * (i % 2):2 * (i % 2) + 2, :].rearrange("p a b -> p (a b)")[:, 0:wd]
                        act.activation(prob[:, i % 2, 0:wd], s_in, ACT.Exp, bias=a_nm[:, i:i + 1],
                                       scale=1.0 if kind == "A" else -1.0,
                                       accum_out=a_den[:, i:i + 1]).then_inc(p_ready, 1)
                    n4, first = divmod(i + 1 - 8 * (HA + HB), 4)
                    if first == 0 and 0 <= n4 < 2 * HC:
                        act.wait_ge(biasc_in[n4 % 2], (l * HC + n4 // 2 + 1) * 16)
                        bias = biasC[n4 % 2][:, :, :]
                        act.activation(bias, bias, ACT.Copy, scale=-1.0).then_inc(biasc_neg, 1)
                    if i >= 9 and (i - 9) % 4 == 0 and (i - 9) // 4 < NB:
                        b = (i - 9) // 4
                        act.wait_ge(pv_done, l * NB + b + 1)
                        kind = ITEMS[4 * b][0]
                        if kind != "C":
                            if b >= 2:
                                act.wait_ge(mg_done, l * NMG + merges_before(b - 1))
                            act.activation(oT[:, (b % 2) * 512:(b % 2 + 1) * 512], ps[:, 6 + b % 2, :], ACT.Copy)\
                               .then_inc(ot_ready, 1)
                        else:
                            act.wait_ge(mg_done, l * NMG + merges_before(b - b % 2))
                            for c in range(2):
                                cb = 2 * (b % 2) + c
                                src = ps[:, 6 + b % 2, c * 256:(c + 1) * 256].rearrange("p (r c) -> p r c", c=16)
                                dst = oT[:, :].rearrange("p (r c) -> p r c", c=GRID_W)[:, :, 16 * cb:16 * cb + 16]
                                act.activation(dst, src, ACT.Copy)
                            act.drain().then_inc(ot_ready, 1)
                barrier(act, l, 1)

                for hf in range(2):
                    split_job(l, "o0", hf)
                norm(l, ST, O, [(0, HA * HD), (HA * HD, (HA + HB) * HD), ((HA + HB) * HD, DM)], lambda t: None)
                for hf in range(2):
                    split_job(l, "o1", hf)
                first = frees_before(len(ACCS) - ST, False)
                norm(l, 2 * ST, x, [(0, DM)], lambda t: act.wait_ge(acc_free_dve, l * DVE_FREE_N + first + t + 1))
                act.wait_ge(acc_done, (l + 1) * len(ACCS))

                def hi_up(u, g_first):
                    act.activation(w_up[:, HI, :, :].rearrange("p k n -> p (k n)"), raw[:, u, :], ACT.Copy)\
                       .then_inc(split_hi, 1)

                def hi_down(u):
                    act.activation(w_dn[:, HI, :, :].rearrange("p k n -> p (k n)"), raw[:, u, :], ACT.Copy)\
                       .then_inc(split_hi, 1)

                def raw_wait(u):
                    act.wait_ge(raw_in[u[1]], (l * (NU // 2) + MLP0 // 2 + u[0] + 1) * 16)

                def relus(tile0):
                    for k in range(4):
                        act.wait_ge(up_tile, tile0 + k + 1)
                        act.wait_ge(hid_ready, tile0 + k - 1 + 2)
                        act.activation(rbuf[:, k % 2, :], ps[:, k, :], ACT.Relu).then_inc(relu_done, 1)

                raw_wait((0, 0))
                hi_up(0, True)
                relus(l * 4 * NG)
                raw_wait((0, 1))
                act.wait_ge(up_tile, l * 4 * NG + 4)
                hi_up(1, False)
                with act.Fori(0, NG - 2) as g:
                    act.wait_ge(down_tile, l * 16 * NG + 16 * g + 16)
                    raw_wait((g + 1, 0))
                    hi_down(0)
                    relus(l * 4 * NG + 4 * g + 4)
                    act.wait_ge(up_tile, l * 4 * NG + 4 * g + 8)
                    raw_wait((g + 1, 1))
                    hi_up(1, False)
                act.wait_ge(down_tile, l * 16 * NG + 16 * (NG - 1))
                raw_wait((NG - 1, 0))
                hi_down(0)
                relus(l * 4 * NG + 4 * (NG - 1))
                act.wait_ge(down_tile, (l + 1) * 16 * NG)
                raw_wait((NG - 1, 1))
                hi_down(1)
                barrier(act, l, 2)

            for t in range(ST):
                if t:
                    act.wait_ge(fin_ready, t)
                if t >= 2:
                    act.wait_ge(fin_out[t % 2], 16 * (t // 2))
                act.activation(hn[:, t % 2, :], x[:, t, :], ACT.Square, scale=float(DM) ** -0.5,
                               accum_out=st_ss[:, 0:1])
                act.drain()
                act.activation(st_sd[:, 0:1], st_ss[:, 0:1], ACT.Sqrt, bias=eps[:, 0:1]).then_inc(sd_ready, 1)

        @block.vector
        def _(dve):
            dve.sem_inc(split_lo, 2)
            dve.sem_inc(gain_free, 1)
            dve.sem_inc(nt_free, 2)
            dve.sem_inc(down_free, 4)
            dve.sem_inc(hid_ready, 2)
            dve.wait_ge(const_in, 16 * 4)

            def rest(out_lo, full, hi):
                return dve.tensor_tensor(out_lo, full, words(hi), ALU.subtract)

            def split_job(l, job, half):
                j = JOBS.index(job)
                u = unit_of(job, half)
                n = unit_len(job, half)
                off = half * unit_len(job, 0)
                dve.wait_ge(split_hi, l * NU + u + 1)
                s = ws[j % 2]
                rest(s[:, LO, off:off + n], raw[:, u % 2, 0:n], s[:, HI, off:off + n]).then_inc(split_lo, 1)

            def norm(l, base, src, groups, gain_no):
                dve.wait_ge(gain_in, (l * 3 + gain_no + 1) * 16)
                for t in range(ST + 1):
                    if t < ST:
                        dve.wait_ge(sd_ready, l * N_HN + base + t + 1)
                        dve.reciprocal(st_rs[:, 0:len(groups)], st_sd[:, 0:len(groups)])
                        dve.drain()
                        for k, (a, b) in enumerate(groups):
                            ins = dve.scalar_tensor_tensor(hn[:, t % 2, a:b], src[:, t, a:b], st_rs[:, k:k + 1],
                                                           gB[:, a:b], ALU.mult, ALU.mult)
                        dve.drain().then_inc(hn_ready, 1)
                        if t == ST - 1:
                            dve.drain().then_inc(gain_free, 1)
                    if t:
                        for hf in range(2):
                            n = 2 * (base + t - 1) + hf
                            dve.wait_ge(nt_hi, l * TN + n + 1)
                            cols = slice((t - 1) * P, t * P)
                            rest(hT[:, LO, 4 * hf:4 * hf + 4, cols],
                                 ps[:, 6 + hf, :].rearrange("p (k s) -> p k s", s=P),
                                 hT[:, HI, 4 * hf:4 * hf + 4, cols]).then_inc(nt_free, 1)

            def rope(dst, src, s, nh, half, scale):
                a = hn[:, 0, 0:nh * 2 * half].rearrange("p (h k d) -> p h k d", k=2, d=half)
                b = hn[:, 1, 0:nh * 2 * half].rearrange("p (h k d) -> p h k d", k=2, d=half)
                v = src.rearrange("p (h k d) -> p h k d", k=2, d=half)
                o = dst.rearrange("p (h k d) -> p h k d", k=2, d=half)
                step = 32 // half
                for k in range(2):
                    c, sn = (tb[:, s, ::step].unsqueeze(1).to_broadcast([P, nh, half]) for tb in (cos, sin))
                    dve.scalar_tensor_tensor(a[:, :, k, :], v[:, :, k, :], scale, c, ALU.mult, ALU.mult)
                    dve.scalar_tensor_tensor(b[:, :, k, :], v[:, :, k, :], scale, sn, ALU.mult, ALU.mult)
                dve.drain()
                dve.tensor_tensor(o[:, :, 0, :], a[:, :, 0, :], b[:, :, 1, :], ALU.subtract)
                return dve.tensor_tensor(o[:, :, 1, :], b[:, :, 0, :], a[:, :, 1, :], ALU.add)

            with dve.Fori(0, DEPTH) as l:
                for hf in range(2):
                    split_job(l, "a", hf)
                norm(l, 0, x, [(0, DM)], 0)
                for hf in range(2):
                    split_job(l, "bq", hf)
                dve.wait_ge(gl_in, (l + 1) * 16)
                acc = turn = stg = vt = st_turn = 0
                for e in EVENTS:
                    if e[0] == "split":
                        split_job(l, e[1], e[2])
                    elif e[0] == "acc":
                        kind, s = e[1], e[2]
                        bank = ps[:, acc % 4, :]
                        wd = width_of(kind)
                        if kind == "a":
                            if s == 0:
                                dve.wait_ge(nt_done, l * TN + 2 * ST)
                            dve.wait_ge(lat_sd, l * ST + s + 1)
                            dve.reciprocal(sl_rs[:, s % 2, :], sl_sd[:, s % 2, :])
                            dve.drain()
                            dve.scalar_tensor_tensor(lat[:, s, 0:QL], lat[:, s, 0:QL], sl_rs[:, s % 2, 0:1],
                                                     gL[:, 0:QL], ALU.mult, ALU.mult)
                            dve.scalar_tensor_tensor(lat[:, s, QL:QL + KVL], lat[:, s, QL:QL + KVL],
                                                     sl_rs[:, s % 2, 1:2], gL[:, QL:QL + KVL], ALU.mult, ALU.mult)
                            rope(lat[:, s, QL + KVL:CA], lat[:, s, QL + KVL:CA], s, 1, RA // 2, 1.0)
                            dve.drain().then_inc(lat_ready, 1)
                        elif kind in ("bq", "bk", "ur"):
                            dve.wait_ge(acc_done, l * len(ACCS) + acc + 1)
                            if stg == 0:
                                dve.wait_ge(parked, (l + 1) * 16 * ST)
                            if stg >= NSTG:
                                dve.wait_ge(turn_done, l * len(TURNS) + turn_of(stg - NSTG) + 1)
                            dst = stage[:, stg % NSTG, :]
                            if kind == "ur":
                                rope(dst[:, 0:wd], bank[:, 0:wd], s, HA, RA // 2, (HD + RA) ** -0.5)
                                dve.tensor_copy(dst[:, wd:wd + RA], lat[:, s, QL + KVL:CA])
                            else:
                                rope(dst[:, 0:wd], bank[:, 0:wd], s, HB, HD // 2, -HD ** -0.5 if kind == "bq" else 1.0)
                            dve.drain().then_inc(acc_free_dve, 1)
                        elif e in VSTAGED:
                            dve.wait_ge(v_hi, l * len(VSTAGED) + vt + 1)
                            nh = wd // HD
                            rest(vst[:, vt % 2, 0:nh, HD:2 * HD], bank[:, 0:wd].rearrange("p (h d) -> p h d", d=HD),
                                 vst[:, vt % 2, 0:nh, 0:HD])
                            dve.drain().then_inc(acc_free_dve, 1)
                            vt += 1
                        if e in STAGED:
                            stg += 1
                        acc += 1
                    else:
                        bank = ps[:, 4 + turn % NTB, :]
                        nj = len(TURN[e[1]][0])
                        dve.wait_ge(turn_hi, l * len(TURNS) + turn + 1)
                        if e[1] == "lat":
                            rest(latT[:, e[2] % 2, LO, :, :], bank[:, 0:3 * P].rearrange("p (k s) -> p k s", s=P),
                                 latT[:, e[2] % 2, HI, :, :]).then_inc(turn_lo, 1)
                        else:
                            k = st_turn % NTS
                            if e[1] == "ur":
                                rest(tst[:, k, LO, 0, :], bank[:, 0:P], tst[:, k, HI, 0, :])
                                rest(tst[0:96, k, LO, 1, :], bank[0:96, P:2 * P], tst[0:96, k, HI, 1, :])
                                dve.drain().then_inc(turn_lo, 1)
                            elif e[1] == "cqk":
                                for j in range(2):
                                    dve.tensor_tensor(by_block(tst[:, k, LO, j, :]), from_grid(bank, j),
                                                      by_block(words(tst[:, k, HI, j, :])), ALU.subtract)
                                rest(tst[:, k, LO, 2:4, :], bank[:, 2 * P:4 * P].rearrange("p (k s) -> p k s", s=P),
                                     tst[:, k, HI, 2:4, :])
                                dve.drain().then_inc(turn_lo, 1)
                            else:
                                rest(tst[:, k, LO, 0:nj, :], bank[:, 0:nj * P].rearrange("p (k s) -> p k s", s=P),
                                     tst[:, k, HI, 0:nj, :]).then_inc(turn_lo, 1)
                            st_turn += 1
                        turn += 1
                barrier(dve, l, 0)

                dve.wait_ge(tab_in, (l + 1) * 16 * 5)
                for i in range(NI + 12):
                    if i < NI:
                        kind, h, q = ITEMS[i]
                        wd = CW if kind == "C" else SEQ
                        dve.wait_ge(s_done, l * NI + i + 1)
                        s_in = ps[:, 2 * (i % 2):2 * (i % 2) + 2, :].rearrange("p a b -> p (a b)")[:, 0:wd]
                        if kind == "A":
                            dve.tensor_reduce(a_nm[:, i:i + 1], s_in, axis=AX.X, op=ALU.max, negate=True)\
                               .then_inc(mx_ready, 1)
                        else:
                            if kind == "B":
                                bias = tabB[:, 896 - P * q:896 - P * q + SEQ]
                            else:
                                n4 = (i - 8 * (HA + HB)) // 4
                                dve.wait_ge(biasc_neg, l * 2 * HC + n4 + 1)
                                bias = biasC[n4 % 2][:, q % 4, :]
                            hold(dve)
                            dve.tensor_tensor_reduce(out=s_in, in0=s_in, in1=bias, scale=1.0, scalar=-NEG,
                                                     op0=ALU.add, op1=ALU.min, accum_out=a_nm[:, i:i + 1])\
                               .then_inc(mx_ready, 1)
                    if 1 <= i <= NI and ITEMS[i - 1][0] == "C":
                        it = i - 1
                        dve.wait_ge(p_ready, l * NI + it + 1)
                        dve.reciprocal(a_rd[:, it:it + 1], a_den[:, it:it + 1])
                        dve.drain()
                        dve.tensor_scalar(prob[:, it % 2, 0:CW], prob[:, it % 2, 0:CW], a_rd[:, it:it + 1], None,
                                          ALU.mult).then_inc(pn_ready, 1)
                    if 2 <= i < NI + 2:
                        it = i - 2
                        b = it // 4
                        for g in ITEM_GROUPS[it]:
                            dve.wait_ge(t_hi, l * NGR + g + 1)
                            nk, k0 = group_keys(g)
                            cols = slice((it % 4) * P, (it % 4 + 1) * P)
                            rest(pT[:, b % 2, LO, k0:k0 + nk, cols],
                                 ps[:, 4 + g % 2, 0:nk * P].rearrange("p (k s) -> p k s", s=P),
                                 pT[:, b % 2, HI, k0:k0 + nk, cols]).then_inc(t_lo, 1)
                    if i >= 12 and (i - 12) % 4 == 0 and merged((i - 12) // 4):
                        b = (i - 12) // 4
                        kind, h, q = ITEMS[4 * b]
                        dve.wait_ge(mg_done, l * NMG + merges_before(b + 1))
                        cols = slice(h * HD, (h + 1) * HD)
                        if kind == "C":
                            dve.tensor_copy(O[:, :, cols],
                                            ps[:, 6 + b % 2, :].rearrange("p (t d) -> p t d", d=HD))\
                               .then_inc(o_ready, 1)
                        else:
                            dve.reciprocal(a_rd[:, 4 * b:4 * b + 4], a_den[:, 4 * b:4 * b + 4])
                            dve.drain()
                            dve.tensor_tensor(O[:, q:q + 4, cols],
                                              ps[:, 6 + b % 2, 0:4 * HD].rearrange("p (t d) -> p t d", d=HD),
                                              a_rd[:, 4 * b:4 * b + 4].unsqueeze(2).to_broadcast([P, 4, HD]),
                                              ALU.mult).then_inc(o_ready, 1)
                barrier(dve, l, 1)

                for hf in range(2):
                    split_job(l, "o0", hf)
                norm(l, ST, O, [(0, HA * HD), (HA * HD, (HA + HB) * HD), ((HA + HB) * HD, DM)], 1)
                for hf in range(2):
                    split_job(l, "o1", hf)
                acc = len(ACCS) - 2 * ST

                def residual(l, acc, nh, s):
                    dve.wait_ge(acc_done, l * len(ACCS) + acc + 1)
                    cols = slice(nh * 512, nh * 512 + 512)
                    dve.tensor_tensor(x[:, s, cols], ps[:, acc % 4, :], x[:, s, cols], ALU.add)\
                       .then_inc(acc_free_dve, 1)

                dve.wait_ge(x_back, (l + 1) * 16 * ST)
                for s in range(ST):
                    residual(l, acc + s, 0, s)
                dve.wait_ge(gain_in, (l * 3 + 3) * 16)
                for t in range(ST + 2):
                    if t < ST:
                        residual(l, acc + ST + t, 1, t)
                    if 1 <= t <= ST:
                        n = t - 1
                        dve.wait_ge(sd_ready, l * N_HN + 2 * ST + n + 1)
                        dve.reciprocal(st_rs[:, 0:1], st_sd[:, 0:1])
                        dve.drain()
                        dve.scalar_tensor_tensor(hn[:, n % 2, :], x[:, n, :], st_rs[:, 0:1], gB[:, :],
                                                 ALU.mult, ALU.mult).then_inc(hn_ready, 1)
                        if n == ST - 1:
                            dve.drain().then_inc(gain_free, 1)
                    if t >= 2:
                        n = t - 2
                        for hf in range(2):
                            m = 2 * (2 * ST + n) + hf
                            dve.wait_ge(nt_hi, l * TN + m + 1)
                            cols = slice(n * P, (n + 1) * P)
                            rest(hT[:, LO, 4 * hf:4 * hf + 4, cols],
                                 ps[:, 6 + hf, :].rearrange("p (k s) -> p k s", s=P),
                                 hT[:, HI, 4 * hf:4 * hf + 4, cols]).then_inc(nt_free, 1)

                def lo_up(u, n):
                    dve.wait_ge(split_hi, l * NU + MLP0 + n + 1)
                    rest(w_up[:, LO, :, :].rearrange("p k n -> p (k n)"), raw[:, u, :],
                         w_up[:, HI, :, :].rearrange("p k n -> p (k n)")).then_inc(split_lo, 1)

                def lo_down(u, n):
                    dve.wait_ge(split_hi, l * NU + MLP0 + n + 1)
                    rest(w_dn[:, LO, :, :].rearrange("p k n -> p (k n)"), raw[:, u, :],
                         w_dn[:, HI, :, :].rearrange("p k n -> p (k n)")).then_inc(split_lo, 1)

                def hidden(tile0, slot, free):
                    for k in range(4):
                        dve.wait_ge(relu_done, tile0 + k + 1)
                        if k == 0 and free is not None:
                            dve.wait_ge(down_tile, free + 16)
                        dve.tensor_tensor(vbuf[:, k % 2, :], rbuf[:, k % 2, :], rbuf[:, k % 2, :], ALU.mult)
                        dve.drain()
                        ft, sh = k // 2, k % 2
                        cols = slice(sh * 512, sh * 512 + 512)
                        dve.tensor_copy(hid[:, slot, HI, ft, cols], vbuf[:, k % 2, :])
                        dve.drain()
                        rest(hid[:, slot, LO, ft, cols], vbuf[:, k % 2, :], hid[:, slot, HI, ft, cols])\
                            .then_inc(hid_ready, 1)

                def residuals(tile0):
                    for s in range(ST):
                        for nh in range(2):
                            m = 2 * s + nh
                            dve.wait_ge(down_tile, tile0 + m + 1 + 16)
                            cols = slice(nh * 512, nh * 512 + 512)
                            dve.tensor_tensor(x[:, s, cols], ps[:, 4 + m % 4, :], x[:, s, cols], ALU.add)\
                               .then_inc(down_free, 1)

                t_up, t_dn = l * 4 * NG, l * 16 * NG
                lo_up(0, 0)
                hidden(t_up, 0, None)
                lo_up(1, 1)
                with dve.Fori(0, NG // 2 - 1) as gg:
                    for k in range(2):
                        lo_down(0, 4 * gg + 2 * k + 2)
                        hidden(t_up + 8 * gg + 4 * k + 4, (k + 1) % 2, t_dn + 32 * gg + 16 * k)
                        lo_up(1, 4 * gg + 2 * k + 3)
                        residuals(t_dn + 32 * gg + 16 * k)
                lo_down(0, 2 * NG - 2)
                hidden(t_up + 4 * (NG - 1), (NG - 1) % 2, t_dn + 16 * (NG - 2))
                residuals(t_dn + 16 * (NG - 2))
                lo_down(1, 2 * NG - 1)
                residuals(t_dn + 16 * (NG - 1))
                barrier(dve, l, 2)

            dve.wait_ge(gain_in, (DEPTH * 3 + 1) * 16)
            for t in range(ST):
                dve.wait_ge(sd_ready, DEPTH * N_HN + t + 1)
                dve.reciprocal(st_rs[:, 0:1], st_sd[:, 0:1])
                dve.drain()
                dve.scalar_tensor_tensor(hn[:, t % 2, :], x[:, t, :], st_rs[:, 0:1], gB[:, :], ALU.mult, ALU.mult)\
                   .then_inc(fin_ready, 1)

        @block.tensor
        def _(pe):
            pe.sem_inc(down_tile, 16)
            pe.wait_ge(const_in, 16 * 4)
            PASSES = ((HI, HI), (HI, LO), (LO, HI))

            def norm_turn(l, base, t):
                pe.wait_ge(hn_ready, l * N_HN + base + t + 1)
                for hf in range(2):
                    n = 2 * (base + t) + hf
                    pe.wait_ge(nt_free, l * TN + n + 1)
                    for k in range(4):
                        last = pe.transpose(ps[:, 6 + hf, k * P:(k + 1) * P],
                                            hn[:, t % 2, (4 * hf + k) * P:(4 * hf + k + 1) * P], ident[:, :])
                    last.then_inc(nt_done, 1)

            def acc_wait(l, acc):
                if acc >= 4:
                    if ACCS[acc - 4][1] in ACT_FREES:
                        pe.wait_ge(acc_free_act, l * ACT_FREE_N + frees_before(acc - 3, True))
                    else:
                        pe.wait_ge(acc_free_dve, l * DVE_FREE_N + frees_before(acc - 3, False))

            def project(l, acc, kind, s):
                job = JOB_OF.get(kind, kind)
                j = JOBS.index(job)
                if (s == 0 and kind != "ur" and kind != "uk" and kind != "uv"):
                    pe.wait_ge(split_lo, l * NU + unit_of(job, 1) + 1 + 2)
                acc_wait(l, acc)
                wd = width_of(kind)
                out_ = ps[:, acc % 4, 0:wd]
                mms = []
                if job == "up":
                    for w1, w2 in PASSES:
                        for (kt, _), (_, wv) in zip(up_views(kind, w1), up_views(kind, w2)):
                            mms.append((latT[:, s % 2, w1, kt, :], wv))
                else:
                    for kt in range(KT):
                        for w1, w2 in PASSES:
                            mms.append((hT[:, w1, kt, s * P:(s + 1) * P], w_view(job, w2)[:, kt, :]))
                for n, (a, b) in enumerate(mms):
                    last = pe.matmul(out_, a, b, start=(n == 0), stop=(n == len(mms) - 1))
                last.then_inc(acc_done, 1)

            with pe.Fori(0, DEPTH) as l:
                norm_turn(l, 0, 0)
                norm_turn(l, 0, 1)
                acc = turn = 0
                for e in EVENTS:
                    if e[0] == "acc":
                        kind, s = e[1], e[2]
                        if kind == "a":
                            pe.wait_ge(nt_free, l * TN + 2 * (s + 1) + 2)
                        if kind == "uq":
                            pe.wait_ge(turn_lo, l * len(TURNS) + TURNS.index(("turn", "lat", s)) + 1)
                        project(l, acc, kind, s)
                        if kind == "a" and 2 * s + 3 < ST:
                            norm_turn(l, 0, 2 * s + 2)
                            norm_turn(l, 0, 2 * s + 3)
                        acc += 1
                    elif e[0] == "turn":
                        kind, s = e[1], e[2]
                        if turn >= NTB:
                            pe.wait_ge(turn_lo, l * len(TURNS) + turn - NTB + 1)
                        if kind == "lat":
                            pe.wait_ge(lat_ready, l * ST + s + 1)
                            src = lat[:, s, :]
                        else:
                            se = ("acc", kind, s)
                            n = ACCS.index(se)
                            if kind in ACT_FREES:
                                pe.wait_ge(acc_free_act, l * ACT_FREE_N + frees_before(n + 1, True))
                            else:
                                pe.wait_ge(acc_free_dve, l * DVE_FREE_N + frees_before(n + 1, False))
                            src = stage[:, STAGED.index(se) % NSTG, :]
                        for j, wd in enumerate(TURN[kind][0]):
                            last = pe.transpose(ps[0:wd, 4 + turn % NTB, j * P:(j + 1) * P], src[:, j * P:j * P + wd],
                                                ident[:, :])
                        last.then_inc(turn_done, 1)
                        turn += 1
                barrier(pe, l, 0)

                pe.wait_ge(tab_in, (l + 1) * 16 * 5)

                def scores(i):
                    kind, h, q = ITEMS[i]
                    n = i // 8
                    hb = head[n % 2]
                    if i % 8 == 0:
                        done = sum(HEAD_DMAS[kd] for kd, _ in HEADS[n % 2:n + 1:2])
                        pe.wait_ge(head_in[n % 2], (l * HEAD_N[n % 2] + done) * 16)
                    if i >= 2:
                        pe.wait_ge(p_ready, l * NI + i - 1)
                    b0 = 2 * (i % 2)
                    if kind == "C":
                        cb, hf = q // 2, q % 2
                        grid = [hb[:, c * 1024:(c + 1) * 1024].rearrange("p (r c) -> p r c", c=GRID_W)
                                for c in range(3)]
                        qt = hb[:, 256 * cb + P * hf:256 * cb + P * (hf + 1)]
                        r0, c0 = key_row0(hf), c_cols(cb)
                        mm = [(qt, grid[1 + w][:, r0:r0 + CKR, c0:c0 + CKC]) for w in range(2)]
                        for k, (a, b) in enumerate(mm):
                            last = pe.matmul(ps[:, b0, 0:CW], a, b, start=(k == 0), stop=(k == 1))
                    else:
                        for kh in range(2):
                            cols = slice(kh * 512, kh * 512 + 512)
                            qt = hb[:, q * P:(q + 1) * P]
                            mm = [(qt, hb[:, 1024 * (1 + w):1024 * (2 + w)][:, cols]) for w in range(2)]
                            if kind == "A":
                                mm.append((hb[:, 3072 + q * P:3072 + (q + 1) * P], kR[:, cols]))
                            for k, (a, b) in enumerate(mm):
                                last = pe.matmul(ps[:, b0 + kh, :], a, b, start=(k == 0), stop=(k == len(mm) - 1))
                    last.then_inc(s_done, 1)

                def turns(i):
                    kind, h, q = ITEMS[i]
                    if kind == "C":
                        pe.wait_ge(pn_ready, l * 8 * HC + i - 8 * (HA + HB) + 1)
                    else:
                        pe.wait_ge(p_ready, l * NI + i + 1)
                    for k, g in enumerate(ITEM_GROUPS[i]):
                        if g >= 2:
                            pe.wait_ge(t_lo, l * NGR + g - 1)
                        nk, _ = group_keys(g)
                        for j in range(nk):
                            c = (4 * k + j) * P
                            last = pe.transpose(ps[:, 4 + g % 2, j * P:(j + 1) * P], prob[:, i % 2, c:c + P],
                                                ident[:, :])
                        last.then_inc(t_done, 1)

                def weigh(b, part):
                    kind, h, q = ITEMS[4 * b]
                    hb = head[(b // 2) % 2]
                    bank = ps[:, 6 + b % 2, :]
                    if part == 0:
                        pe.wait_ge(t_lo, l * NGR + ITEM_GROUPS[4 * b + 3][-1] + 1)
                        n, k = b // 2, b // 2 % 2
                        done = sum(VALUE_DMAS[kd] for kd, _ in HEADS[k:n + 1:2])
                        pe.wait_ge(value_in[k], (l * VALUE_N[k] + done) * 16)
                        if b >= 2:
                            pe.wait_ge(o_ready, l * NMG + merges_before(b - 1))
                            pe.wait_ge(ot_ready, l * NB + b - 1)
                    if kind == "C":
                        c, w = part // 2, part % 2
                        cb = q // 2 + c
                        for n, (g, a, z) in enumerate(((1, 0, 256), (2, 0, 256), (0, 0, 128), (3, 128, 256))):
                            v = hb[:, 3072 + (4 * cb + g) * P:3072 + (4 * cb + g + 1) * P]
                            last = pe.matmul(bank[:, c * 256 + a:c * 256 + z], v,
                                             pT[:, b % 2, w, g, c * 256 + a:c * 256 + z],
                                             start=(w == 0 and n == 0), stop=(w == 1 and n == 3),
                                             skip_group_check=True)
                    else:
                        for kt in (2 * part, 2 * part + 1):
                            for w in range(2):
                                last = pe.matmul(bank, hb[:, 4096 + kt * P:4096 + (kt + 1) * P],
                                                 pT[:, b % 2, w, kt, :], start=(part == 0 and kt == 0 and w == 0),
                                                 stop=(part == 3 and kt == 7 and w == 1))
                    if part == 3:
                        last.then_inc(pv_done, 1)

                def merge(b):
                    kind, h, q = ITEMS[4 * b]
                    pe.wait_ge(ot_ready, l * NB + b + 1)
                    for k in range(8 if kind == "C" else 4):
                        c = k * P + (0 if kind == "C" else (b % 2) * 512)
                        last = pe.matmul(ps[:, 6 + b % 2, k * HD:(k + 1) * HD], oT[:, c:c + P], pair[:, :],
                                         start=True, stop=True)
                    last.then_inc(mg_done, 1)

                for i in range(NI + 12):
                    if i < NI:
                        scores(i)
                    if 2 <= i < NI + 2:
                        turns(i - 2)
                    if i >= 11 and (i - 11) % 4 == 0 and merged((i - 11) // 4):
                        merge((i - 11) // 4)
                    if i >= 6 and (i - 6) // 4 < NB:
                        weigh((i - 6) // 4, (i - 6) % 4)
                barrier(pe, l, 1)

                norm_turn(l, ST, 0)
                norm_turn(l, ST, 1)
                for s in range(ST):
                    pe.wait_ge(nt_free, l * TN + 2 * (ST + s + 1) + 2)
                    project(l, acc, "o0", s)
                    acc += 1
                    if 2 * s + 3 < ST:
                        norm_turn(l, ST, 2 * s + 2)
                        norm_turn(l, ST, 2 * s + 3)
                for s in range(ST):
                    project(l, acc, "o1", s)
                    acc += 1
                    if s >= 2:
                        norm_turn(l, 2 * ST, s - 2)
                norm_turn(l, 2 * ST, ST - 2)
                norm_turn(l, 2 * ST, ST - 1)
                pe.wait_ge(nt_free, (l + 1) * TN + 2)
                pe.wait_ge(acc_free_dve, (l + 1) * DVE_FREE_N)

                def up(g, unit, first):
                    pe.wait_ge(split_lo, l * NU + MLP0 + unit + 1 + 2)
                    for ft in range(FT):
                        for sh in range(2):
                            k = 2 * ft + sh
                            if not first:
                                pe.wait_ge(relu_done, l * 4 * NG + 4 * g + k - 3)
                            for kt in range(KT):
                                for w1, w2 in PASSES:
                                    last = pe.matmul(ps[:, k, :], w_up[:, w1, kt, ft * P:(ft + 1) * P],
                                                     hT[:, w2, kt, sh * 512:(sh + 1) * 512],
                                                     start=(kt == 0 and (w1, w2) == PASSES[0]),
                                                     stop=(kt == KT - 1 and (w1, w2) == PASSES[-1]))
                            last.then_inc(up_tile, 1)

                def down(g, slot, unit):
                    pe.wait_ge(split_lo, l * NU + MLP0 + unit + 1 + 2)
                    pe.wait_ge(hid_ready, l * 4 * NG + 4 * g + 4 + 2)
                    for s in range(ST):
                        for nh in range(2):
                            m = 2 * s + nh
                            pe.wait_ge(down_free, l * 16 * NG + 16 * g + m + 1)
                            for ft in range(FT):
                                for w1, w2 in PASSES:
                                    last = pe.matmul(ps[:, 4 + m % 4, :], hid[:, slot, w1, ft, s * P:(s + 1) * P],
                                                     w_dn[:, w2, ft, nh * 512:(nh + 1) * 512],
                                                     start=(ft == 0 and (w1, w2) == PASSES[0]),
                                                     stop=(ft == FT - 1 and (w1, w2) == PASSES[-1]))
                            last.then_inc(down_tile, 1)

                up(0, 0, True)
                with pe.Fori(0, NG // 2 - 1) as gg:
                    for k in range(2):
                        up(2 * gg + k + 1, 4 * gg + 2 * k + 1, False)
                        down(2 * gg + k, k, 4 * gg + 2 * k + 2)
                up(NG - 1, 2 * NG - 3, False)
                down(NG - 2, 0, 2 * NG - 2)
                down(NG - 1, 1, 2 * NG - 1)
                barrier(pe, l, 2)


def stores_of(e):
    return 6 if e[1] == "cqk" else 2


TST_N = [sum(stores_of(e) for e in STORED[k::NTS]) for k in range(NTS)]
TST_BEFORE = [sum(stores_of(e) for e in STORED[n % NTS:n:NTS]) for n in range(len(STORED))]
HEAD_DMAS = {"A": 6 + 4, "B": 6, "C": 6}
VALUE_DMAS = {"A": 1, "B": 1, "C": 16}
HEAD_N = [sum(HEAD_DMAS[kd] for kd, _ in HEADS[k::2]) for k in range(2)]
VALUE_N = [sum(VALUE_DMAS[kd] for kd, _ in HEADS[k::2]) for k in range(2)]
MERGED = [ITEMS[4 * b][0] != "C" or b % 2 == 1 for b in range(NB)]
NMG = sum(MERGED)


def merged(b):
    return b < NB and MERGED[b]


def merges_before(b):
    return sum(MERGED[:b])


def turn_of(stg):
    e = STAGED[stg]
    return TURNS.index(("turn", e[1], e[2]))


def group_keys(g):
    it, half = GROUPS[g]
    kind, h, q = ITEMS[it]
    return (3, q % 2) if kind == "C" else (4, 4 * half)


def _pack_unit(w, n0):
    import numpy as np
    r, n = w.shape
    flat = np.ascontiguousarray(w.reshape(r // P, P, n).transpose(1, 0, 2)).reshape(P, -1)
    full = np.zeros((P, ULEN), np.float32)
    full[:, :flat.shape[1]] = flat
    return full


def _weight_stream(w_in, w_uq, w_ukv, w_out, w1, w2):
    import numpy as np
    ca, cb = CA, 3 * HB * HD
    b0, c0 = ca, ca + cb
    cols = {"a": (0, ca), "bq": (b0, b0 + 384), "bk": (b0 + 384, b0 + 768), "bv": (b0 + 768, b0 + 1152),
            "cqk": (c0, c0 + 512), "cv": (c0 + 512, c0 + 768)}
    out = np.zeros((DEPTH, NU, P, ULEN), np.float32)
    for l in range(DEPTH):
        for job, (a, b) in cols.items():
            for hf in range(2):
                out[l, 2 * JOBS.index(job) + hf] = _pack_unit(w_in[l, hf * 512:hf * 512 + 512, a:b], 0)
        uq = w_uq[l].reshape(QL, HA, HD + RA)
        uq = np.concatenate([uq[:, :, :HD].reshape(QL, -1), uq[:, :, HD:].reshape(QL, -1)], axis=1)
        ukv = w_ukv[l].reshape(KVL, HA, 2 * HD)
        ukv = np.concatenate([ukv[:, :, :HD].reshape(KVL, -1), ukv[:, :, HD:].reshape(KVL, -1)], axis=1)
        u = 2 * JOBS.index("up")
        out[l, u] = _pack_unit(uq, 0)
        out[l, u + 1] = _pack_unit(ukv, 0)
        for n in range(2):
            for hf in range(2):
                out[l, 2 * JOBS.index(f"o{n}") + hf] = _pack_unit(
                    w_out[l, hf * 512:hf * 512 + 512, n * 512:n * 512 + 512], 0)
        for g in range(NG):
            out[l, up_unit(g)] = _pack_unit(w1[l, :, g * FG:(g + 1) * FG], 0)
            out[l, down_unit(g)] = _pack_unit(w2[l, g * FG:(g + 1) * FG, :], 0)
    return out


def _rotary():
    import numpy as np
    half = HD // 2
    inv = (np.float32(10000.0) ** (-np.arange(half, dtype=np.float32) / np.float32(half))).astype(np.float32)
    ang = np.arange(SEQ, dtype=np.float32)[:, None] * inv[None, :]
    shape = lambda a: np.ascontiguousarray(a.astype(np.float32).reshape(ST, P, half).transpose(1, 0, 2))
    return shape(np.cos(ang)), shape(np.sin(ang))


def _bias_b():
    import numpy as np
    d = np.arange(P)[:, None] + 896 - np.arange(1920)[None, :]
    n = ((abs(d) <= 64).astype(int) + ((d % 4 == 0) & (abs(d) <= 256)) + (d % 16 == 0))
    return np.where(n > 0, -np.log(np.maximum(n, 1)), -NEG).astype(np.float32)


def _bias_c(rpb):
    import numpy as np
    item = np.arange(8)
    cb, hf = item // 2, item % 2
    p, k = np.arange(P), np.arange(CW)
    rq = 8 * hf[:, None] + p[None, :] // 16
    cq = 16 * cb[:, None] + p[None, :] % 16
    rk = 4 * hf[:, None] + k[None, :] // CKC
    ck = np.array([c_cols(c) for c in cb])[:, None] + k[None, :] % CKC
    rs = np.clip(rq - 4, 0, ROWS - 8)[:, :, None]
    cs = np.clip(cq - 8, 0, GRID_W - 16)[:, :, None]
    rk, ck, rq, cq = rk[:, None, :], ck[:, None, :], rq[:, :, None], cq[:, :, None]
    ok = (rk >= rs) & (rk < rs + 8) & (ck >= cs) & (ck < cs + 16)
    dr = np.clip(rk - rq, -7, 7) + 7
    dc = np.clip(ck - cq, -15, 15) + 15
    full = np.where(ok[None, None], rpb[:, :, dr, dc], np.float32(NEG)).astype(np.float32)
    return np.ascontiguousarray(full.reshape(DEPTH, HC, 2, 4, P, CW).transpose(0, 1, 2, 4, 3, 5))


def kernel(**inputs):
    import numpy as np
    import concourse.bacc as bacc
    from concourse.bass_utils import run_bass_kernel_spmd

    a = {k: np.asarray(v) for k, v in inputs.items()}

    def wide(v):
        return np.ascontiguousarray(np.broadcast_to(v[..., None, :], v.shape[:-1] + (P, v.shape[-1])))

    cos, sin = _rotary()
    eye = np.eye(P, dtype=np.float32)
    out_gain = np.concatenate([a["out_norm_a"], a["out_norm_b"], a["out_norm_c"]], axis=-1)
    arrays = {
        "x": np.ascontiguousarray(a["x"][0]),
        "wstream": _weight_stream(a["w_in"], a["w_uq"], a["w_ukv"], a["w_out"], a["w_mlp_in"], a["w_mlp_out"]),
        "gains": wide(np.stack([a["g_mix"], out_gain, a["g_mlp"]], axis=1)),
        "lat_gains": wide(np.concatenate([a["q_norm"], a["kv_norm"]], axis=-1)),
        "cos": cos, "sin": sin, "bias_b": _bias_b(), "bias_c": _bias_c(a["rpb"]),
        "ident": eye, "pair": np.concatenate([np.eye(HD, dtype=np.float32)] * 2, axis=0),
        "g_final": wide(a["g_final"]),
    }
    nc = bacc.Bacc("TRN2", target_bir_lowering=False, num_devices=1)
    arrays = {f"in_{k}": v for k, v in arrays.items()}
    args = [nc.dram_tensor(k, v.shape, mybir.dt.from_np(v.dtype), kind="ExternalInput").ap()
            for k, v in arrays.items()]
    out = nc.dram_tensor("out", (SEQ, DM), mybir.dt.float32, kind="ExternalOutput").ap()
    encoder(nc, *args, out)
    r = run_bass_kernel_spmd(nc, [arrays], core_ids=[0])
    return r.results[0]["out"].reshape(1, SEQ, DM)
```

```python
import concourse.bass as bass
from concourse import mybir
from contextlib import ExitStack

P = 128
DEPTH = 2
SEQ = 1024
DM = 1024
DFF = 4096
HD = 64
HA, HB, HC = 6, 6, 4
NH = HA + HB + HC
QL, KVL, RA = 256, 128, 32
GRID_W = 64
ROWS = SEQ // GRID_W
EPS = 1e-6
NEG = -1e30

ST = SEQ // P
KT = DM // P
HI, LO = 0, 1

CA = QL + KVL + RA
WIDTH = {"a": CA, "bq": HB * HD, "up": None, "bk": HB * HD, "bv": HB * HD, "cqk": 2 * HC * HD, "cv": HC * HD,
         "o0": DM // 2, "o1": DM // 2}
JOBS = list(WIDTH)
NJ = len(JOBS)
SLOT = {job: (j if j < NJ - 2 else j - NJ + 2) % 2 for j, job in enumerate(JOBS)}
UQ_N, UQ_R, UK_N, UV_N = HA * HD, HA * RA, HA * HD, HA * HD
UQ = UQ_N + UQ_R
UKV = UK_N + UV_N

ULEN = 2048
FG = 256
NG = DFF // FG
FT = FG // P
MLP0 = 2 * NJ
NU = MLP0 + 2 * NG


def up_unit(g):
    return MLP0 + (2 * g - 1 if g else 0)


def down_unit(g):
    return MLP0 + (2 * g + 2 if g < NG - 1 else 2 * NG - 1)


def unit_len(job, half):
    if job == "up":
        return (2 * UQ, UKV)[half]
    return KT // 2 * WIDTH[job]


F_AQ, F_AK = 0, UQ_N
F_BQ, F_BK = F_AK + UK_N, F_AK + UK_N + HB * HD
F_CQ = F_BK + HB * HD
F_CK = F_CQ + HC * HD
F_AR = F_CK + HC * HD
NF = F_AR + UQ_R + RA

CKR, CKC = 12, 32
CW = CKR * CKC


def c_cols(cb):
    return min(max(16 * cb - 8, 0), GRID_W - CKC)


def key_row0(half):
    return 4 * half


HEADS = [("A", h) for h in range(HA)] + [("B", HA + h) for h in range(HB)] + [("C", HA + HB + h) for h in range(HC)]
ITEMS = [(kind, h, i) for kind, h in HEADS for i in range(8)]
NI = len(ITEMS)
NB = NI // 4
GROUPS = []
ITEM_GROUPS = []
for n_, (kind_, _, _) in enumerate(ITEMS):
    ITEM_GROUPS.append([])
    for half_ in range(1 if kind_ == "C" else 2):
        ITEM_GROUPS[-1].append(len(GROUPS))
        GROUPS.append((n_, half_))
NGR = len(GROUPS)


def schedule():
    ev = []

    def split(job):
        return [("split", job, 0), ("split", job, 1)]

    for s in range(ST):
        ev.append(("acc", "a", s))
    for s in range(ST - 2):
        ev.append(("acc", "bq", s))
        if s:
            ev.append(("turn", "bq", s - 1))
        if s == 1:
            ev += split("up")
        if s == ST - 4:
            ev.append(("turn", "lat", 0))
    fill = {0: ("bq", ST - 2), 1: ("bq", ST - 1), **{s + 3: ("bk", s) for s in range(ST)}}
    turned = ("bq", ST - 3)
    for s in range(ST + 3):
        if s < ST:
            ev += [("acc", "uq", s), ("acc", "ur", s)]
        if turned and s <= ST:
            ev.append(("turn", *turned))
        if 1 <= s <= ST:
            ev.append(("turn", "uk", s - 1))
        if s < ST - 1:
            ev.append(("turn", "lat", s + 1))
        before, turned = turned, fill.get(s)
        if turned:
            ev.append(("acc", *turned))
        if s > ST:
            ev.append(("turn", *before))
        if s == ST:
            ev += split("bv")
        if s < ST:
            ev += [("turn", "uq", s), ("turn", "ur", s), ("acc", "uk", s), ("acc", "uv", s)]
        if s == 1 or s == 2:
            ev.append(("split", "bk", s - 1))
    for s in range(ST):
        ev.append(("acc", "bv", s))
        if s == 0:
            ev.append(("turn", "bk", ST - 1))
        if s == 1:
            ev += split("cqk")
    for s in range(ST):
        ev.append(("acc", "cqk", s))
        if s:
            ev.append(("turn", "cqk", s - 1))
        if s == 1:
            ev += split("cv")
    for s in range(ST):
        ev.append(("acc", "cv", s))
        if s == 1:
            ev.append(("turn", "cqk", ST - 1))
    return ev


EVENTS = schedule()
JOB_OF = {"uq": "up", "ur": "up", "uk": "up", "uv": "up"}
OUT_TILES = [("acc", o, s) for o in ("o0", "o1") for s in range(ST)]
ACCS = [e for e in EVENTS if e[0] == "acc"] + OUT_TILES
ACT_FREES = ("a", "uq", "uk", "cqk")
TURNS = [e for e in EVENTS if e[0] == "turn"]


def job_end(job):
    return max(n for n, e in enumerate(ACCS) if JOB_OF.get(e[1], e[1]) == job) + 1


STAGED = [e for e in ACCS if e[1] in ("bq", "bk", "uq", "ur", "uk", "cqk")]
VSTAGED = [e for e in ACCS if e[1] in ("uv", "bv", "cv")]
NSTG = 4
NTB = 4
NTS = 3
TURN = {"bq": ([P] * 3, F_BQ), "bk": ([P] * 3, F_BK), "uq": ([P] * 3, F_AQ), "uk": ([P] * 3, F_AK),
        "ur": ([P, 96], F_AR), "cqk": ([P] * 4, F_CQ), "lat": ([P] * 3, None)}
STORED = [e for e in TURNS if e[1] != "lat"]


def frees_before(n, act):
    return sum((e[1] in ACT_FREES) == act for e in ACCS[:n])


ACT_FREE_N, DVE_FREE_N = frees_before(len(ACCS), True), frees_before(len(ACCS), False)


def encoder(nc, x_in, wstream, gains, lat_gains, cos_in, sin_in, bias_b, bias_c, ident_in, pair_in, out):
    f32, f32r = mybir.dt.float32, mybir.dt.float32r
    ALU, ACT, AX = mybir.AluOpType, mybir.ActivationFunctionType, mybir.AxisListType

    feats = nc.dram_tensor("feats", [2, NF, SEQ], f32).ap()
    values = nc.dram_tensor("values", [SEQ, NH * 2 * HD], f32).ap()
    x_park = nc.dram_tensor("x_park", [ST, P, DM], f32).ap()

    KB = 1024
    at = {}
    top = (nc.sbuf_base + 31) // 32 * 32
    for name, size in [("R0", 32 * KB), ("H", 64 * KB), ("WS", 64 * KB), ("RAW", 16 * KB), ("HN", 8 * KB),
                       ("LAT", 13312), ("ROPE", 2 * KB), ("ID", 512 + 256), ("GB", 4 * KB), ("GL", 1536),
                       ("STAT", 2304 + 64)]:
        at[name] = top
        top += size

    def sb(name, shape, dt, region, offset=0):
        return nc.alloc_sbuf_tensor_at(name, shape, dt, offset=at[region] + offset)

    x = sb("x", [P, ST, DM], f32, "R0")
    hT = sb("hT", [P, 2, KT, SEQ], f32r, "H")
    ws = [sb(f"ws{k}", [P, 2, 4096], f32r, "WS", k * 32 * KB) for k in range(2)]
    w_up = [sb(f"w_up{k}", [P, 2, KT, FG], f32r, "WS", 32 * k * KB) for k in range(2)]
    w_dn = [sb(f"w_dn{k}", [P, 2, FT, DM], f32r, "WS", 32 * k * KB) for k in range(2)]
    hid = [sb(f"hid{k}", [P, 2, FT, SEQ], f32r, "WS", (16 + 32 * k) * KB) for k in range(2)]
    raw = sb("raw", [P, 2, ULEN], f32, "RAW")
    hn = sb("hn", [P, 2, DM], f32, "HN")
    lat = sb("lat", [P, ST, CA], f32, "LAT")
    cos = sb("cos", [P, ST, 32], f32, "ROPE")
    sin = sb("sin", [P, ST, 32], f32, "ROPE", KB)
    ident = sb("ident", [P, P], f32, "ID")
    pair = sb("pair", [P, HD], f32, "ID", 512)
    gB = sb("gB", [P, DM], f32, "GB")
    gL = sb("gL", [P, QL + KVL], f32, "GL")
    st_ss = sb("st_ss", [P, 4], f32, "STAT")
    st_sd = sb("st_sd", [P, 4], f32, "STAT", 32)
    st_rs = sb("st_rs", [P, 4], f32, "STAT", 64)
    sl_ss = sb("sl_ss", [P, 2, 2], f32, "STAT", 96)
    sl_sd = sb("sl_sd", [P, 2, 2], f32, "STAT", 128)
    sl_rs = sb("sl_rs", [P, 2, 2], f32, "STAT", 160)
    eps = sb("eps", [P, 1], f32, "STAT", 192)
    a_nm = sb("a_nm", [P, NI], f32, "STAT", 256 + 512)
    a_den = sb("a_den", [P, NI], f32, "STAT", 256 + 1024)
    a_rd = sb("a_rd", [P, NI], f32, "STAT", 256 + 1536)
    tst = sb("tst", [P, NTS, 2, 4, P], f32r, "R0")
    latT = sb("latT", [P, 2, 2, 3, P], f32r, "R0", 12 * KB)
    vst = sb("vst", [P, 2, 6, 2 * HD], f32r, "R0", 18 * KB)
    stage = sb("stage", [P, NSTG, 512], f32, "R0", 24 * KB)
    O = sb("O", [P, ST, DM], f32, "R0")
    head = [sb(f"head{k}", [P, 5 * 1024], f32r, "WS", (32 - 32 * k) * KB) for k in range(2)]
    kR = sb("kR", [P, SEQ], f32r, "WS", 52 * KB)
    prob = sb("prob", [P, 2, 1024], f32, "WS", 20 * KB)
    oT = sb("oT", [P, 1024], f32, "WS", 28 * KB)
    biasC = [sb("biasC0", [P, 4, CW], f32, "HN"), sb("biasC1", [P, 4, CW], f32, "WS", 56 * KB)]
    tabB = sb("tabB", [P, 1920], f32, "LAT")
    pT = sb("pT", [P, 2, 2, 8, 512], f32r, "H")
    rbuf = sb("rbuf", [P, 2, 512], f32, "HN")
    vbuf = sb("vbuf", [P, 2, 512], f32, "HN", 4 * KB)

    ctx = ExitStack()
    with ctx:
        ps = ctx.enter_context(nc.psum_tensor("ps", [P, 8, 512], f32))

        def sem(name):
            return ctx.enter_context(nc.semaphore(name))

        const_in = sem("const_in")
        eps_set = sem("eps_set")
        ident_loaded = sem("ident_loaded")
        x_loaded = [sem(f"x_loaded{t}") for t in range(ST)]
        gain_in = sem("gain_in")
        gl_in = sem("gl_in")
        gain_free = sem("gain_free")
        raw_in = [sem(f"raw_in{k}") for k in range(2)]
        split_hi = sem("split_hi")
        split_lo = sem("split_lo")
        ss_ready, sd_ready, hn_ready = sem("ss_ready"), sem("sd_ready"), sem("hn_ready")
        nt_done, nt_hi, nt_free = sem("nt_done"), sem("nt_hi"), sem("nt_free")
        acc_done = sem("acc_done")
        acc_free_act, acc_free_dve = sem("acc_free_act"), sem("acc_free_dve")
        lat_sd, lat_ready = sem("lat_sd"), sem("lat_ready")
        turn_done, turn_hi, turn_lo = sem("turn_done"), sem("turn_hi"), sem("turn_lo")
        v_hi = sem("v_hi")
        tst_out = [sem(f"tst_out{k}") for k in range(NTS)]
        vst_out = [sem(f"vst_out{k}") for k in range(2)]
        parked = sem("parked")
        tab_in, kr_in = sem("tab_in"), sem("kr_in")
        head_in = [sem(f"head_in{k}") for k in range(2)]
        value_in = [sem(f"value_in{k}") for k in range(2)]
        biasc_neg = sem("biasc_neg")
        biasc_in = [sem(f"biasc_in{k}") for k in range(2)]
        s_done, mx_ready, p_ready, pn_ready = sem("s_done"), sem("mx_ready"), sem("p_ready"), sem("pn_ready")
        t_done, t_hi, t_lo = sem("t_done"), sem("t_hi"), sem("t_lo")
        pv_done, ot_ready, mg_done, o_ready = sem("pv_done"), sem("ot_ready"), sem("mg_done"), sem("o_ready")
        up_tile, relu_done, hid_ready = sem("up_tile"), sem("relu_done"), sem("hid_ready")
        down_tile, down_free = sem("down_tile"), sem("down_free")
        fin_ready = sem("fin_ready")
        fin_out = [sem(f"fin_out{k}") for k in range(2)]

        TN = 3 * 2 * ST
        N_HN = 3 * ST

        passed = sem("passed")

        def hold(eng):
            eng.sem_inc(passed, 1)

        def starting(l):
            return isinstance(l, int)

        def unit_of(job, half):
            return 2 * JOBS.index(job) + half

        def w_view(job, w):
            s = ws[SLOT[job]]
            return s[:, w, 0:KT * WIDTH[job]].rearrange("p (k n) -> p k n", n=WIDTH[job])

        def up_views(kind, w):
            s = ws[SLOT["up"]]
            uq = s[:, w, 0:2 * UQ].rearrange("p (k n) -> p k n", n=UQ)
            ukv = s[:, w, 2 * UQ:2 * UQ + UKV]
            return {"uq": [(0, uq[:, 0, 0:UQ_N]), (1, uq[:, 1, 0:UQ_N])],
                    "ur": [(0, uq[:, 0, UQ_N:UQ]), (1, uq[:, 1, UQ_N:UQ])],
                    "uk": [(2, ukv[:, 0:UK_N])], "uv": [(2, ukv[:, UK_N:UKV])]}[kind]

        def width_of(kind):
            return {"uq": UQ_N, "ur": UQ_R, "uk": UK_N, "uv": UV_N}.get(kind) or WIDTH[kind]

        def words(ap):
            return ap.bitcast(f32)

        def from_grid(bank, j):
            return bank[:, j * P:(j + 1) * P].rearrange("p (r b c) -> p b r c", r=2, b=4)

        def by_block(ap):
            return ap.rearrange("p (b r c) -> p b r c", r=2, b=4)

        block = ctx.enter_context(nc.Block())

        @block.sync
        def _(sp):
            sp.dma_start(x[:, 0, :], x_in[0:P, :]).then_inc(x_loaded[0], 16)
            sp.dma_start(ident[:, :], ident_in).then_inc(ident_loaded, 16)
            sp.dma_start(gB[:, :], gains[0]).then_inc(gain_in, 16)
            for t in range(1, ST):
                sp.dma_start(x[:, t, :], x_in[t * P:(t + 1) * P, :]).then_inc(x_loaded[t], 16)
                if t in (3, 5):
                    u = t // 2 - 1
                    length = unit_len("a", u)
                    sp.dma_start(raw[:, u, 0:length], wstream[u, :, 0:length]).then_inc(raw_in[u], 16)
            sp.dma_start(pair[:, :], pair_in).then_inc(const_in, 16)
            sp.dma_start(cos[:, :, :], cos_in).then_inc(const_in, 16)
            sp.dma_start(sin[:, :, :], sin_in).then_inc(const_in, 16)
            for k in range(2):
                sp.sem_inc(fin_out[k], 16 * (ST // 2))

            def load_unit(l, u, length=ULEN):
                sp.wait_ge(split_lo, l * NU + u + 1)
                hold(sp)
                sp.dma_start(raw[:, u % 2, 0:length], wstream[l * NU + u, :, 0:length]).then_inc(raw_in[u % 2], 16)

            def load_gain(l, k):
                sp.wait_ge(gain_free, l * 3 + k)
                hold(sp)
                sp.dma_start(gB[:, :], gains[l * 3 + k]).then_inc(gain_in, 16)

            def load_head(l, n):
                kind, h = HEADS[n]
                load_features(l, n)
                if kind == "C":
                    load_bias(l, 2 * (h - HA - HB))
                load_values(l, n)
                if kind == "C":
                    load_bias(l, 2 * (h - HA - HB) + 1)

            def load_bias(l, nc_half):
                if nc_half >= 2:
                    sp.wait_ge(mx_ready, l * NI + 8 * (HA + HB) + 4 * (nc_half - 1))
                sp.dma_start(biasC[nc_half % 2][:, :, :], bias_c[l, nc_half // 2, nc_half % 2])\
                  .then_inc(biasc_in[nc_half % 2], 16)

            def load_features(l, n):
                kind, h = HEADS[n]
                k = n % 2
                if n >= 2:
                    sp.wait_ge(s_done, l * NI + 8 * (n - 1))
                hb = words(head[k][:, :])
                kh = h if kind == "A" else h - HA if kind == "B" else h - HA - HB
                fq = {"A": F_AQ, "B": F_BQ, "C": F_CQ}[kind] + kh * HD
                fk = {"A": F_AK, "B": F_BK, "C": F_CK}[kind] + kh * HD
                for part in range(2):
                    rows = slice(64 * part, 64 * part + 64)
                    sp.dma_start(hb[rows, 0:1024], feats[part, fq:fq + HD, :]).then_inc(head_in[k], 16)
                    for w in range(2):
                        sp.dma_start(hb[rows, 1024 * (1 + w):1024 * (2 + w)], feats[w, fk:fk + HD, :])\
                          .then_inc(head_in[k], 16)
                if kind == "A":
                    for q, w in enumerate((HI, HI, LO, LO)):
                        sp.dma_start(hb[32 * q:32 * q + 32, 3072:4096],
                                     feats[w, F_AR + kh * RA:F_AR + (kh + 1) * RA, :]).then_inc(head_in[k], 16)

            def load_values(l, n):
                kind, h = HEADS[n]
                k = n % 2
                hb = words(head[k][:, :])
                if n >= 2:
                    sp.wait_ge(pv_done, l * NB + 2 * (n - 1))
                if kind != "C":
                    sp.dma_start(hb[:, 4096:5120].rearrange("p (t d) -> p t d", d=P),
                                 values[:, h * P:(h + 1) * P].rearrange("(t p) d -> p t d", p=P))\
                      .then_inc(value_in[k], 16)
                else:
                    grid = values.rearrange("(r c) d -> r c d", c=GRID_W)
                    for cb in range(4):
                        for rr in range(4):
                            dst = hb[32 * rr:32 * rr + 32, 3072 + 512 * cb:3072 + 512 * (cb + 1)]
                            src = grid[rr:rr + 13:4, c_cols(cb):c_cols(cb) + CKC, h * P:(h + 1) * P]
                            sp.dma_start(dst.rearrange("c (g d) -> c g d", d=P),
                                         src.rearrange("g c d -> c g d")).then_inc(value_in[k], 16)

            def stores_done(l):
                for k in range(NTS):
                    sp.wait_ge(tst_out[k], (l + 1) * 16 * TST_N[k])
                    hold(sp)
                for k in range(2):
                    sp.wait_ge(vst_out[k], (l + 1) * 16 * (len(VSTAGED) // 2))
                    hold(sp)

            def first_head(l, s, turn, vt):
                if s == 0:
                    sp.wait_ge(acc_done, l * len(ACCS) + job_end("cqk"))
                    hold(sp)
                    for k in range(NTS):
                        sp.wait_ge(tst_out[k], (l * TST_N[k] + stores_before(k, turn)) * 16)
                        hold(sp)
                    for k in range(2):
                        sp.wait_ge(vst_out[k], (l * (len(VSTAGED) // 2) + (vt - k + 1) // 2) * 16)
                        hold(sp)
                    for q, w in enumerate((HI, LO, HI, LO)):
                        sp.dma_start(words(kR[32 * q:32 * q + 32, :]), feats[w, F_AR + UQ_R:F_AR + UQ_R + RA, :])\
                          .then_inc(kr_in, 16)
                    load_features(l, 0)
                elif s == 1:
                    load_values(l, 0)

            with sp.Fori(0, DEPTH) as l:
                sp.dma_start(gL[:, :], lat_gains[l]).then_inc(gl_in, 16)
                for u in (2, 3):
                    load_unit(l, u, unit_len(JOBS[u // 2], u % 2))
                for t in range(ST):
                    sp.wait_ge(hn_ready, l * N_HN + t + 1)
                    sp.dma_start(x_park[t], x[:, t, :]).then_inc(parked, 16)
                load_gain(l, 1)
                for u in (4, 5):
                    load_unit(l, u, unit_len(JOBS[u // 2], u % 2))
                turn = vt = 0
                for e in EVENTS:
                    if e[0] == "acc" and e[1] == "cv":
                        first_head(l, e[2], turn, vt)
                    if e[0] == "split":
                        u = unit_of(e[1], e[2]) + 2
                        load_unit(l, u, unit_len(JOBS[u // 2], u % 2))
                    elif e in STORED:
                        n = TURNS.index(e)
                        k = turn % NTS
                        sp.wait_ge(turn_lo, l * len(TURNS) + n + 1)
                        cols = slice(e[2] * P, (e[2] + 1) * P)
                        widths, f0 = TURN[e[1]]
                        if e[1] == "ur":
                            for j, wd in enumerate(widths):
                                sp.dma_start(feats[:, f0 + j * P:f0 + j * P + wd, cols].rearrange("w p s -> p w s"),
                                             words(tst[0:wd, k, :, j, :])).then_inc(tst_out[k], 16)
                        elif e[1] == "cqk":
                            r = 2 * P // GRID_W * 8
                            for w in range(2):
                                for j in range(2):
                                    sp.dma_start(
                                        feats[w, F_CQ + j * P:F_CQ + (j + 1) * P, :]
                                        .rearrange("p (b s) -> p b s", b=4)[:, :, r * e[2]:r * (e[2] + 1)],
                                        words(tst[:, k, w, j, :]).rearrange("p (b s) -> p b s", b=4))\
                                      .then_inc(tst_out[k], 16)
                                sp.dma_start(
                                    feats[w, F_CK:F_CK + 2 * P, cols].rearrange("(j p) s -> p j s", p=P),
                                    words(tst[:, k, w, 2:4, :])).then_inc(tst_out[k], 16)
                        else:
                            nj = len(widths)
                            for w in range(2):
                                sp.dma_start(
                                    feats[w, f0:f0 + nj * P, cols].rearrange("(j p) s -> p j s", p=P),
                                    words(tst[:, k, w, 0:nj, :])).then_inc(tst_out[k], 16)
                        turn += 1
                    elif e in VSTAGED:
                        vt += 1
                sp.wait_ge(acc_done, l * len(ACCS) + job_end("cv"))
                hold(sp)

                for n in range(1, NH):
                    if n == 2:
                        stores_done(l)
                        sp.dma_start(tabB[:, :], bias_b).then_inc(tab_in, 16)
                    load_head(l, n)

                for t in range(ST):
                    sp.wait_ge(hn_ready, l * N_HN + ST + t + 1)
                    sp.dma_start(x[:, t, :], x_park[t]).then_inc(x_loaded[t], 16)
                    if t == 1:
                        load_unit(l, 16)
                        load_unit(l, 17)
                load_gain(l, 2)
                with sp.Fori(0, NG) as g:
                    load_unit_pair = l * NU + MLP0 + 2 * g
                    for k in range(2):
                        sp.wait_ge(split_lo, load_unit_pair + k + 1)
                        hold(sp)
                        sp.dma_start(raw[:, k, :], wstream[l * NU + MLP0 + 2 * g + k]).then_inc(raw_in[k], 16)
                load_gain(l, 3)
                for u in range(2):
                    load_unit(l, NU + u, unit_len("a", u))
                for t in range(ST):
                    sp.wait_ge(hn_ready, l * N_HN + 3 * ST + t + 1)
                    sp.dma_start(out[t * P:(t + 1) * P, :], hn[:, t % 2, :]).then_inc(fin_out[t % 2], 16)
            for k in range(2):
                sp.wait_ge(fin_out[k], 16 * (ST // 2) * (DEPTH + 1))

        @block.gpsimd
        def _(pool):
            pool.memset(eps[:, :], EPS).then_inc(eps_set, 1)
            with pool.Fori(0, DEPTH) as l:
                for vt, e in enumerate(VSTAGED):
                    k = vt % 2
                    pool.wait_ge(acc_free_dve, l * DVE_FREE_N + frees_before(ACCS.index(e) + 1, False))
                    hold(pool)
                    h0, nh = {"uv": (0, HA), "bv": (HA, HB), "cv": (HA + HB, HC)}[e[1]]
                    pool.dma_start(values[e[2] * P:(e[2] + 1) * P, h0 * P:(h0 + nh) * P],
                                   words(vst[:, k, 0:nh, :].rearrange("p h d -> p (h d)"))).then_inc(vst_out[k], 16)

        @block.scalar
        def _(act):
            act.wait_ge(eps_set, 1)

            def use_table(func):
                act.activation(st_sd[:, 3:4], eps[:, 0:1], func)

            use_table(ACT.Sqrt)

            def split_unit(l, u, dst):
                act.wait_ge(raw_in[u % 2], (l * (NU // 2) + u // 2 + 1) * 16)
                act.activation(dst, raw[:, u % 2, 0:dst.shape[-1]], ACT.Copy).then_inc(split_hi, 1)

            def split_job(l, job, half):
                j = JOBS.index(job)
                if 2 <= j < 7:
                    act.wait_ge(acc_done, l * len(ACCS) + job_end(JOBS[j - 2]))
                off = half * unit_len(job, 0)
                split_unit(l, unit_of(job, half), ws[SLOT[job]][:, HI, off:off + unit_len(job, half)])

            def norm_stats(l, base, t, src, groups):
                if t or not starting(l):
                    act.wait_ge(hn_ready, l * N_HN + base + t)
                for k, (a, b) in enumerate(groups):
                    act.activation(hn[:, t % 2, a:b], src[:, t, a:b], ACT.Square, scale=float(b - a) ** -0.5,
                                   accum_out=st_ss[:, k:k + 1])
                act.drain()
                act.activation(st_sd[:, 0:len(groups)], st_ss[:, 0:len(groups)], ACT.Sqrt, bias=eps[:, 0:1])\
                   .then_inc(sd_ready, 1)

            def norm_hi(l, base, t):
                for hf in range(2):
                    n = 2 * (base + t) + hf
                    act.wait_ge(nt_done, l * TN + n + 1)
                    act.activation(hT[:, HI, 4 * hf:4 * hf + 4, t * P:(t + 1) * P],
                                   ps[:, 6 + hf, :].rearrange("p (k s) -> p k s", s=P), ACT.Copy).then_inc(nt_hi, 1)

            def norm(l, base, src, groups, before):
                for t in range(ST + 1):
                    if t < ST:
                        before(t)
                        if t >= 2:
                            act.wait_ge(nt_done, l * TN + 2 * (base + t - 1))
                            if base == 3 * ST and not starting(l):
                                act.wait_ge(fin_out[t % 2], ((l + 1) * (ST // 2) + t // 2) * 16)
                        norm_stats(l, base, t, src, groups)
                    if t:
                        norm_hi(l, base, t - 1)

            def split_a(l, half):
                off = half * unit_len("a", 0)
                split_unit(l, NU + half, ws[SLOT["a"]][:, HI, off:off + unit_len("a", half)])

            def first_x(t):
                act.wait_ge(x_loaded[t], 16)
                if t in (5, 7):
                    split_a(-1, t // 2 - 2)

            norm(-1, 3 * ST, x, [(0, DM)], first_x)
            with act.Fori(0, DEPTH) as l:
                act.wait_ge(down_tile, l * 16 * NG + 16)
                for hf in range(2):
                    split_job(l, "bq", hf)
                acc = turn = stg = vt = st_turn = 0
                for e in EVENTS:
                    if e == ("acc", "bv", 0):
                        use_table(ACT.Exp)
                    if e[0] == "split":
                        split_job(l, e[1], e[2])
                    elif e[0] == "acc":
                        kind, s = e[1], e[2]
                        bank = ps[:, acc % 4, :]
                        wd = width_of(kind)
                        if kind == "a":
                            act.wait_ge(acc_done, l * len(ACCS) + acc + 1)
                            act.activation(lat[:, s, :], bank[:, 0:CA], ACT.Copy)
                            act.drain()
                            if s >= 2:
                                act.wait_ge(lat_ready, l * ST + s - 1)
                            act.activation(bank[:, 0:QL], bank[:, 0:QL], ACT.Square, scale=float(QL) ** -0.5,
                                           accum_out=sl_ss[:, s % 2, 0:1])
                            act.activation(bank[:, QL:QL + KVL], bank[:, QL:QL + KVL], ACT.Square,
                                           scale=float(KVL) ** -0.5, accum_out=sl_ss[:, s % 2, 1:2])
                            act.drain().then_inc(acc_free_act, 1)
                            act.activation(sl_sd[:, s % 2, :], sl_ss[:, s % 2, :], ACT.Sqrt, bias=eps[:, 0:1])\
                               .then_inc(lat_sd, 1)
                        elif kind in ("uq", "uk", "cqk"):
                            act.wait_ge(acc_done, l * len(ACCS) + acc + 1)
                            if stg >= NSTG:
                                act.wait_ge(turn_done, l * len(TURNS) + turn_of(stg - NSTG) + 1)
                            dst = stage[:, stg % NSTG, :]
                            if kind == "cqk":
                                act.activation(dst[:, 0:wd // 2], bank[:, 0:wd // 2], ACT.Copy, scale=-HD ** -0.5)
                                act.activation(dst[:, wd // 2:wd], bank[:, wd // 2:wd], ACT.Copy)
                            else:
                                act.activation(dst[:, 0:wd], bank[:, 0:wd], ACT.Copy,
                                               scale=(HD + RA) ** -0.5 if kind == "uq" else 1.0)
                            act.drain().then_inc(acc_free_act, 1)
                        elif e in VSTAGED:
                            act.wait_ge(acc_done, l * len(ACCS) + acc + 1)
                            if vt >= 2:
                                act.wait_ge(vst_out[vt % 2], (l * (len(VSTAGED) // 2) + vt // 2) * 16)
                            elif vt == 0:
                                act.wait_ge(parked, (l + 1) * 16 * ST)
                            nh = wd // HD
                            act.activation(vst[:, vt % 2, 0:nh, 0:HD],
                                           bank[:, 0:wd].rearrange("p (h d) -> p h d", d=HD), ACT.Copy)\
                               .then_inc(v_hi, 1)
                            vt += 1
                        if e in STAGED:
                            stg += 1
                        acc += 1
                    else:
                        bank = ps[:, 4 + turn % NTB, :]
                        nj = len(TURN[e[1]][0])
                        act.wait_ge(turn_done, l * len(TURNS) + turn + 1)
                        if turn == 0:
                            act.wait_ge(parked, (l + 1) * 16 * ST)
                        if e[1] == "lat":
                            if e[2] >= 2:
                                act.wait_ge(acc_done, l * len(ACCS) + ACCS.index(("acc", "uv", e[2] - 2)) + 1)
                            act.activation(latT[:, e[2] % 2, HI, :, :],
                                           bank[:, 0:3 * P].rearrange("p (k s) -> p k s", s=P), ACT.Copy)\
                               .then_inc(turn_hi, 1)
                        else:
                            k = st_turn % NTS
                            if st_turn >= NTS:
                                act.wait_ge(tst_out[k], (l * TST_N[k] + TST_BEFORE[st_turn]) * 16)
                            if e[1] == "ur":
                                act.activation(tst[:, k, HI, 0, :], bank[:, 0:P], ACT.Copy)
                                act.activation(tst[0:96, k, HI, 1, :], bank[0:96, P:2 * P], ACT.Copy)
                                act.drain().then_inc(turn_hi, 1)
                            elif e[1] == "cqk":
                                for j in range(2):
                                    act.activation(by_block(tst[:, k, HI, j, :]), from_grid(bank, j), ACT.Copy)
                                act.activation(tst[:, k, HI, 2:4, :],
                                               bank[:, 2 * P:4 * P].rearrange("p (k s) -> p k s", s=P), ACT.Copy)
                                act.drain().then_inc(turn_hi, 1)
                            else:
                                act.activation(tst[:, k, HI, 0:nj, :],
                                               bank[:, 0:nj * P].rearrange("p (k s) -> p k s", s=P), ACT.Copy)\
                                   .then_inc(turn_hi, 1)
                            st_turn += 1
                        turn += 1

                for i in range(NI + 8):
                    if 2 <= i < NI + 2:
                        it = i - 2
                        b = it // 4
                        if it % 4 == 0 and b >= 2:
                            act.wait_ge(pv_done, l * NB + b - 1)
                        for g in ITEM_GROUPS[it]:
                            act.wait_ge(t_done, l * NGR + g + 1)
                            nk, k0 = group_keys(g)
                            act.activation(pT[:, b % 2, HI, k0:k0 + nk, (it % 4) * P:(it % 4 + 1) * P],
                                           ps[:, 4 + g % 2, 0:nk * P].rearrange("p (k s) -> p k s", s=P), ACT.Copy)\
                               .then_inc(t_hi, 1)
                    if i < NI:
                        kind = ITEMS[i][0]
                        wd = CW if kind == "C" else SEQ
                        act.wait_ge(mx_ready, l * NI + i + 1)
                        if i >= 2:
                            act.wait_ge(t_done, l * NGR + ITEM_GROUPS[i - 2][-1] + 1)
                        s_in = ps[:, 2 * (i % 2):2 * (i % 2) + 2, :].rearrange("p a b -> p (a b)")[:, 0:wd]
                        act.activation(prob[:, i % 2, 0:wd], s_in, ACT.Exp, bias=a_nm[:, i:i + 1],
                                       scale=1.0 if kind == "A" else -1.0,
                                       accum_out=a_den[:, i:i + 1]).then_inc(p_ready, 1)
                    if i == NI:
                        use_table(ACT.Sqrt)
                    n4, part = divmod(i + 2 - 8 * (HA + HB), 4)
                    if 0 <= n4 < 2 * HC:
                        if part == 0:
                            act.wait_ge(biasc_in[n4 % 2], (l * HC + n4 // 2 + 1) * 16)
                        bias = biasC[n4 % 2][:, part, :]
                        act.activation(bias, bias, ACT.Copy, scale=-1.0).then_inc(biasc_neg, 1)
                    if i >= 9 and (i - 9) % 4 == 0 and (i - 9) // 4 < NB:
                        b = (i - 9) // 4
                        act.wait_ge(pv_done, l * NB + b + 1)
                        kind = ITEMS[4 * b][0]
                        if kind != "C":
                            if b >= 2:
                                act.wait_ge(mg_done, l * NMG + merges_before(b - 1))
                            act.activation(oT[:, (b % 2) * 512:(b % 2 + 1) * 512], ps[:, 6 + b % 2, :], ACT.Copy)\
                               .then_inc(ot_ready, 1)
                        else:
                            act.wait_ge(mg_done, l * NMG + merges_before(b - b % 2))
                            for c in range(2):
                                cb = 2 * (b % 2) + c
                                src = ps[:, 6 + b % 2, c * 256:(c + 1) * 256].rearrange("p (r c) -> p r c", c=16)
                                dst = oT[:, :].rearrange("p (r c) -> p r c", c=GRID_W)[:, :, 16 * cb:16 * cb + 16]
                                act.activation(dst, src, ACT.Copy)
                            act.drain().then_inc(ot_ready, 1)
                act.wait_ge(o_ready, (l + 1) * NMG)

                def output_weights(t):
                    if t == 2:
                        split_job(l, "o0", 0)
                        split_job(l, "o0", 1)
                    elif t in (4, 5):
                        split_job(l, "o1", t - 4)

                norm(l, ST, O, [(0, HA * HD), (HA * HD, (HA + HB) * HD), ((HA + HB) * HD, DM)], output_weights)

                def hi_up(u, place):
                    act.activation(w_up[place][:, HI, :, :].rearrange("p k n -> p (k n)"), raw[:, u, :], ACT.Copy)\
                       .then_inc(split_hi, 1)

                def hi_down(u, place):
                    act.activation(w_dn[place][:, HI, :, :].rearrange("p k n -> p (k n)"), raw[:, u, :], ACT.Copy)\
                       .then_inc(split_hi, 1)

                def raw_wait(u):
                    act.wait_ge(raw_in[u[1]], (l * (NU // 2) + MLP0 // 2 + u[0] + 1) * 16)

                def relus(tile0, first=False):
                    for k in range(4):
                        if first and k == 1:
                            raw_wait((0, 1))
                            hi_up(1, 1)
                        act.wait_ge(up_tile, tile0 + k + 1)
                        act.wait_ge(hid_ready, tile0 + k - 1 + 2)
                        act.activation(rbuf[:, k % 2, :], ps[:, k % 2, :], ACT.Relu).then_inc(relu_done, 1)

                first = frees_before(len(ACCS) - ST, False)

                def second_norm(t):
                    if t == 1:
                        act.wait_ge(acc_done, l * len(ACCS) + job_end("o0"))
                        raw_wait((0, 0))
                        hi_up(0, 0)
                    act.wait_ge(acc_free_dve, l * DVE_FREE_N + first + t + 1)

                norm(l, 2 * ST, x, [(0, DM)], second_norm)
                relus(l * 4 * NG, first=True)
                with act.Fori(0, NG - 2) as g:
                    act.wait_ge(down_tile, l * 16 * NG + 16 * g + 16)
                    act.wait_ge(up_tile, l * 4 * NG + 4 * g + 4)
                    raw_wait((g + 1, 0))
                    hi_down(0, 0)
                    relus(l * 4 * NG + 4 * g + 4)
                    act.wait_ge(up_tile, l * 4 * NG + 4 * g + 8)
                    raw_wait((g + 1, 1))
                    hi_up(1, 1)
                act.wait_ge(down_tile, l * 16 * NG + 16 * (NG - 1))
                raw_wait((NG - 1, 0))
                hi_down(0, 0)
                relus(l * 4 * NG + 4 * (NG - 1))
                act.wait_ge(up_tile, (l + 1) * 4 * NG)
                raw_wait((NG - 1, 1))
                hi_down(1, 1)
                act.wait_ge(down_tile, (l + 1) * 16 * NG)
                for hf in range(2):
                    split_a(l, hf)
                act.wait_ge(hid_ready, (l + 1) * 4 * NG + 2)
                norm(l, 3 * ST, x, [(0, DM)], lambda t: act.wait_ge(down_free, (l + 1) * 16 * NG - 16 + 2 * t + 2 + 4))

        @block.vector
        def _(dve):
            dve.sem_inc(split_lo, 2)
            dve.sem_inc(nt_free, 2)
            dve.sem_inc(down_free, 4)
            dve.sem_inc(hid_ready, 2)

            def rest(out_lo, full, hi):
                return dve.tensor_tensor(out_lo, full, words(hi), ALU.subtract)

            def split_job(l, job, half):
                j = JOBS.index(job)
                u = unit_of(job, half)
                n = unit_len(job, half)
                off = half * unit_len(job, 0)
                dve.wait_ge(split_hi, l * NU + u + 1)
                s = ws[SLOT[job]]
                rest(s[:, LO, off:off + n], raw[:, u % 2, 0:n], s[:, HI, off:off + n]).then_inc(split_lo, 1)

            def norm_scale(l, base, t, src, groups):
                dve.wait_ge(sd_ready, l * N_HN + base + t + 1)
                dve.reciprocal(st_rs[:, 0:len(groups)], st_sd[:, 0:len(groups)])
                dve.drain()
                for k, (a, b) in enumerate(groups):
                    dve.scalar_tensor_tensor(hn[:, t % 2, a:b], src[:, t, a:b], st_rs[:, k:k + 1], gB[:, a:b],
                                             ALU.mult, ALU.mult)
                dve.drain().then_inc(hn_ready, 1)
                if t == ST - 1:
                    dve.drain().then_inc(gain_free, 1)

            def norm_lo(l, base, t):
                for hf in range(2):
                    dve.wait_ge(nt_hi, l * TN + 2 * (base + t) + hf + 1)
                    cols = slice(t * P, (t + 1) * P)
                    rest(hT[:, LO, 4 * hf:4 * hf + 4, cols], ps[:, 6 + hf, :].rearrange("p (k s) -> p k s", s=P),
                         hT[:, HI, 4 * hf:4 * hf + 4, cols]).then_inc(nt_free, 1)

            def norm(l, base, src, groups, gain_no, before):
                dve.wait_ge(gain_in, (l * 3 + gain_no + 1) * 16)
                for t in range(ST + 1):
                    before(t)
                    if t < ST:
                        norm_scale(l, base, t, src, groups)
                    if t:
                        norm_lo(l, base, t - 1)

            def rope(dst, src, s, nh, half, scale):
                a = hn[:, 0, 0:nh * 2 * half].rearrange("p (h k d) -> p h k d", k=2, d=half)
                b = hn[:, 1, 0:nh * 2 * half].rearrange("p (h k d) -> p h k d", k=2, d=half)
                v = src.rearrange("p (h k d) -> p h k d", k=2, d=half)
                o = dst.rearrange("p (h k d) -> p h k d", k=2, d=half)
                step = 32 // half
                for k in range(2):
                    c, sn = (tb[:, s, ::step].unsqueeze(1).to_broadcast([P, nh, half]) for tb in (cos, sin))
                    dve.scalar_tensor_tensor(a[:, :, k, :], v[:, :, k, :], scale, c, ALU.mult, ALU.mult)
                    dve.scalar_tensor_tensor(b[:, :, k, :], v[:, :, k, :], scale, sn, ALU.mult, ALU.mult)
                dve.drain()
                dve.tensor_tensor(o[:, :, 0, :], a[:, :, 0, :], b[:, :, 1, :], ALU.subtract)
                return dve.tensor_tensor(o[:, :, 1, :], b[:, :, 0, :], a[:, :, 1, :], ALU.add)

            def split_a(l, half):
                n = unit_len("a", half)
                off = half * unit_len("a", 0)
                dve.wait_ge(split_hi, l * NU + NU + half + 1)
                s = ws[SLOT["a"]]
                rest(s[:, LO, off:off + n], raw[:, half, 0:n], s[:, HI, off:off + n]).then_inc(split_lo, 1)

            def first_split(t):
                if t in (5, 7):
                    split_a(-1, t // 2 - 2)

            norm(-1, 3 * ST, x, [(0, DM)], 3, first_split)
            dve.wait_ge(const_in, 16 * 3)
            with dve.Fori(0, DEPTH) as l:
                for hf in range(2):
                    split_job(l, "bq", hf)
                dve.wait_ge(gl_in, (l + 1) * 16)
                acc = turn = stg = vt = st_turn = 0
                for e in EVENTS:
                    if e[0] == "split":
                        split_job(l, e[1], e[2])
                    elif e[0] == "acc":
                        kind, s = e[1], e[2]
                        bank = ps[:, acc % 4, :]
                        wd = width_of(kind)
                        if kind == "a":
                            if s == 0:
                                dve.wait_ge(nt_done, l * TN + 2 * ST)
                                for k in range(2):
                                    dve.wait_ge(fin_out[k], (l + 1) * 16 * (ST // 2))
                            dve.wait_ge(lat_sd, l * ST + s + 1)
                            dve.reciprocal(sl_rs[:, s % 2, :], sl_sd[:, s % 2, :])
                            dve.drain()
                            dve.scalar_tensor_tensor(lat[:, s, 0:QL], lat[:, s, 0:QL], sl_rs[:, s % 2, 0:1],
                                                     gL[:, 0:QL], ALU.mult, ALU.mult)
                            dve.scalar_tensor_tensor(lat[:, s, QL:QL + KVL], lat[:, s, QL:QL + KVL],
                                                     sl_rs[:, s % 2, 1:2], gL[:, QL:QL + KVL], ALU.mult, ALU.mult)
                            rope(lat[:, s, QL + KVL:CA], lat[:, s, QL + KVL:CA], s, 1, RA // 2, 1.0)
                            dve.drain().then_inc(lat_ready, 1)
                        elif kind in ("bq", "bk", "ur"):
                            dve.wait_ge(acc_done, l * len(ACCS) + acc + 1)
                            if stg == 0:
                                dve.wait_ge(parked, (l + 1) * 16 * ST)
                            if stg >= NSTG:
                                dve.wait_ge(turn_done, l * len(TURNS) + turn_of(stg - NSTG) + 1)
                            dst = stage[:, stg % NSTG, :]
                            if kind == "ur":
                                rope(dst[:, 0:wd], bank[:, 0:wd], s, HA, RA // 2, (HD + RA) ** -0.5)
                                dve.tensor_copy(dst[:, wd:wd + RA], lat[:, s, QL + KVL:CA])
                            else:
                                rope(dst[:, 0:wd], bank[:, 0:wd], s, HB, HD // 2, -HD ** -0.5 if kind == "bq" else 1.0)
                            dve.drain().then_inc(acc_free_dve, 1)
                        elif e in VSTAGED:
                            dve.wait_ge(v_hi, l * len(VSTAGED) + vt + 1)
                            nh = wd // HD
                            rest(vst[:, vt % 2, 0:nh, HD:2 * HD], bank[:, 0:wd].rearrange("p (h d) -> p h d", d=HD),
                                 vst[:, vt % 2, 0:nh, 0:HD])
                            dve.drain().then_inc(acc_free_dve, 1)
                            vt += 1
                        if e in STAGED:
                            stg += 1
                        acc += 1
                    else:
                        bank = ps[:, 4 + turn % NTB, :]
                        nj = len(TURN[e[1]][0])
                        dve.wait_ge(turn_hi, l * len(TURNS) + turn + 1)
                        if e[1] == "lat":
                            rest(latT[:, e[2] % 2, LO, :, :], bank[:, 0:3 * P].rearrange("p (k s) -> p k s", s=P),
                                 latT[:, e[2] % 2, HI, :, :]).then_inc(turn_lo, 1)
                        else:
                            k = st_turn % NTS
                            if e[1] == "ur":
                                rest(tst[:, k, LO, 0, :], bank[:, 0:P], tst[:, k, HI, 0, :])
                                rest(tst[0:96, k, LO, 1, :], bank[0:96, P:2 * P], tst[0:96, k, HI, 1, :])
                                dve.drain().then_inc(turn_lo, 1)
                            elif e[1] == "cqk":
                                for j in range(2):
                                    dve.tensor_tensor(by_block(tst[:, k, LO, j, :]), from_grid(bank, j),
                                                      by_block(words(tst[:, k, HI, j, :])), ALU.subtract)
                                rest(tst[:, k, LO, 2:4, :], bank[:, 2 * P:4 * P].rearrange("p (k s) -> p k s", s=P),
                                     tst[:, k, HI, 2:4, :])
                                dve.drain().then_inc(turn_lo, 1)
                            else:
                                rest(tst[:, k, LO, 0:nj, :], bank[:, 0:nj * P].rearrange("p (k s) -> p k s", s=P),
                                     tst[:, k, HI, 0:nj, :]).then_inc(turn_lo, 1)
                            st_turn += 1
                        turn += 1

                for i in range(NI + 12):
                    if i < NI:
                        kind, h, q = ITEMS[i]
                        wd = CW if kind == "C" else SEQ
                        dve.wait_ge(s_done, l * NI + i + 1)
                        s_in = ps[:, 2 * (i % 2):2 * (i % 2) + 2, :].rearrange("p a b -> p (a b)")[:, 0:wd]
                        if kind == "A":
                            dve.tensor_reduce(a_nm[:, i:i + 1], s_in, axis=AX.X, op=ALU.max, negate=True)\
                               .then_inc(mx_ready, 1)
                        else:
                            if kind == "B":
                                dve.wait_ge(tab_in, (l + 1) * 16)
                                bias = tabB[:, 896 - P * q:896 - P * q + SEQ]
                            else:
                                n4 = (i - 8 * (HA + HB)) // 4
                                dve.wait_ge(biasc_neg, l * 8 * HC + i - 8 * (HA + HB) + 1)
                                bias = biasC[n4 % 2][:, q % 4, :]
                            hold(dve)
                            dve.tensor_tensor_reduce(out=s_in, in0=s_in, in1=bias, scale=1.0, scalar=-NEG,
                                                     op0=ALU.add, op1=ALU.min, accum_out=a_nm[:, i:i + 1])\
                               .then_inc(mx_ready, 1)
                    if 1 <= i <= NI and ITEMS[i - 1][0] == "C":
                        it = i - 1
                        dve.wait_ge(p_ready, l * NI + it + 1)
                        dve.reciprocal(a_rd[:, it:it + 1], a_den[:, it:it + 1])
                        dve.drain()
                        dve.tensor_scalar(prob[:, it % 2, 0:CW], prob[:, it % 2, 0:CW], a_rd[:, it:it + 1], None,
                                          ALU.mult).then_inc(pn_ready, 1)
                    if 2 <= i < NI + 2:
                        it = i - 2
                        b = it // 4
                        for g in ITEM_GROUPS[it]:
                            dve.wait_ge(t_hi, l * NGR + g + 1)
                            nk, k0 = group_keys(g)
                            cols = slice((it % 4) * P, (it % 4 + 1) * P)
                            rest(pT[:, b % 2, LO, k0:k0 + nk, cols],
                                 ps[:, 4 + g % 2, 0:nk * P].rearrange("p (k s) -> p k s", s=P),
                                 pT[:, b % 2, HI, k0:k0 + nk, cols]).then_inc(t_lo, 1)
                    if i >= 12 and (i - 12) % 4 == 0 and merged((i - 12) // 4):
                        b = (i - 12) // 4
                        kind, h, q = ITEMS[4 * b]
                        if b == 0:
                            for k in range(NTS):
                                dve.wait_ge(tst_out[k], (l + 1) * 16 * TST_N[k])
                            for k in range(2):
                                dve.wait_ge(vst_out[k], (l + 1) * 16 * (len(VSTAGED) // 2))
                        dve.wait_ge(mg_done, l * NMG + merges_before(b + 1))
                        cols = slice(h * HD, (h + 1) * HD)
                        if kind == "C":
                            dve.tensor_copy(O[:, :, cols],
                                            ps[:, 6 + b % 2, :].rearrange("p (t d) -> p t d", d=HD))\
                               .then_inc(o_ready, 1)
                        else:
                            dve.reciprocal(a_rd[:, 4 * b:4 * b + 4], a_den[:, 4 * b:4 * b + 4])
                            dve.drain()
                            dve.tensor_tensor(O[:, q:q + 4, cols],
                                              ps[:, 6 + b % 2, 0:4 * HD].rearrange("p (t d) -> p t d", d=HD),
                                              a_rd[:, 4 * b:4 * b + 4].unsqueeze(2).to_broadcast([P, 4, HD]),
                                              ALU.mult).then_inc(o_ready, 1)

                acc = len(ACCS) - 2 * ST

                def residual(l, acc, nh, s):
                    if nh == 0:
                        dve.wait_ge(x_loaded[s], (l + 2) * 16)
                    dve.wait_ge(acc_done, l * len(ACCS) + acc + 1)
                    cols = slice(nh * 512, nh * 512 + 512)
                    dve.tensor_tensor(x[:, s, cols], ps[:, acc % 4, :], x[:, s, cols], ALU.add)\
                       .then_inc(acc_free_dve, 1)

                def between(t):
                    if t == 2:
                        split_job(l, "o0", 0)
                        split_job(l, "o0", 1)
                    if t >= 3:
                        residual(l, acc + t - 3, 0, t - 3)
                    if t in (5, 6):
                        split_job(l, "o1", t - 5)

                norm(l, ST, O, [(0, HA * HD), (HA * HD, (HA + HB) * HD), ((HA + HB) * HD, DM)], 1, between)
                for s in range(ST - 2, ST):
                    residual(l, acc + s, 0, s)

                def lo_up(u, n, place):
                    dve.wait_ge(split_hi, l * NU + MLP0 + n + 1)
                    rest(w_up[place][:, LO, :, :].rearrange("p k n -> p (k n)"), raw[:, u, :],
                         w_up[place][:, HI, :, :].rearrange("p k n -> p (k n)")).then_inc(split_lo, 1)

                dve.wait_ge(gain_in, (l * 3 + 3) * 16)
                for t in range(ST + 2):
                    if t < ST:
                        residual(l, acc + ST + t, 1, t)
                    if 1 <= t <= ST:
                        norm_scale(l, 2 * ST, t - 1, x, [(0, DM)])
                    if t == 2:
                        lo_up(0, 0, 0)
                    if t >= 2:
                        norm_lo(l, 2 * ST, t - 2)

                def lo_down(u, n, place):
                    dve.wait_ge(split_hi, l * NU + MLP0 + n + 1)
                    rest(w_dn[place][:, LO, :, :].rearrange("p k n -> p (k n)"), raw[:, u, :],
                         w_dn[place][:, HI, :, :].rearrange("p k n -> p (k n)")).then_inc(split_lo, 1)

                def hidden(tile0, slot, free):
                    for k in range(4):
                        if free is None and k == 1:
                            lo_up(1, 1, 1)
                        dve.wait_ge(relu_done, tile0 + k + 1)
                        if k == 0 and free is not None:
                            dve.wait_ge(down_tile, free + 16)
                        dve.tensor_tensor(vbuf[:, k % 2, :], rbuf[:, k % 2, :], rbuf[:, k % 2, :], ALU.mult)
                        dve.drain()
                        sh, ft = k // 2, k % 2
                        cols = slice(sh * 512, sh * 512 + 512)
                        dve.tensor_copy(hid[slot][:, HI, ft, cols], vbuf[:, k % 2, :])
                        dve.drain()
                        rest(hid[slot][:, LO, ft, cols], vbuf[:, k % 2, :], hid[slot][:, HI, ft, cols])\
                            .then_inc(hid_ready, 1)

                def residual_down(tile0, m):
                    s, nh = m // 2, m % 2
                    dve.wait_ge(down_tile, tile0 + m + 1 + 16)
                    cols = slice(nh * 512, nh * 512 + 512)
                    dve.tensor_tensor(x[:, s, cols], ps[:, 2 + m % 4, :], x[:, s, cols], ALU.add)\
                       .then_inc(down_free, 1)

                def residuals(tile0):
                    for m in range(2 * ST):
                        residual_down(tile0, m)

                t_up, t_dn = l * 4 * NG, l * 16 * NG
                hidden(t_up, 0, None)
                with dve.Fori(0, NG // 2 - 1) as gg:
                    for k in range(2):
                        lo_down(0, 4 * gg + 2 * k + 2, 0)
                        hidden(t_up + 8 * gg + 4 * k + 4, (k + 1) % 2, t_dn + 32 * gg + 16 * k)
                        lo_up(1, 4 * gg + 2 * k + 3, 1)
                        residuals(t_dn + 32 * gg + 16 * k)
                lo_down(0, 2 * NG - 2, 0)
                hidden(t_up + 4 * (NG - 1), (NG - 1) % 2, t_dn + 16 * (NG - 2))
                lo_down(1, 2 * NG - 1, 1)
                residuals(t_dn + 16 * (NG - 2))
                dve.wait_ge(gain_in, (l * 3 + 4) * 16)
                for t in range(ST + 3):
                    if t >= 3:
                        norm_lo(l, 3 * ST, t - 3)
                    if t < ST:
                        for nh in range(2):
                            residual_down(t_dn + 16 * (NG - 1), 2 * t + nh)
                    if t < 2:
                        split_a(l, t)
                    if 1 <= t <= ST:
                        norm_scale(l, 3 * ST, t - 1, x, [(0, DM)])

        @block.tensor
        def _(pe):
            pe.sem_inc(down_tile, 16)
            pe.wait_ge(ident_loaded, 16)
            LEAD = ST - 2
            PASSES = ((HI, HI), (HI, LO), (LO, HI))

            def norm_turn(l, base, t):
                pe.wait_ge(hn_ready, l * N_HN + base + t + 1)
                for hf in range(2):
                    n = 2 * (base + t) + hf
                    pe.wait_ge(nt_free, l * TN + n + 1)
                    for k in range(4):
                        last = pe.transpose(ps[:, 6 + hf, k * P:(k + 1) * P],
                                            hn[:, t % 2, (4 * hf + k) * P:(4 * hf + k + 1) * P], ident[:, :])
                    last.then_inc(nt_done, 1)

            def acc_wait(l, acc):
                if acc >= 4:
                    if ACCS[acc - 4][1] in ACT_FREES:
                        pe.wait_ge(acc_free_act, l * ACT_FREE_N + frees_before(acc - 3, True))
                    else:
                        pe.wait_ge(acc_free_dve, l * DVE_FREE_N + frees_before(acc - 3, False))

            def project(l, acc, kind, s):
                job = JOB_OF.get(kind, kind)
                j = JOBS.index(job)
                if s == 0 and kind != "ur" and kind != "uv":
                    pe.wait_ge(split_lo, l * NU + unit_of(job, kind == "uk") + 1 + 2)
                acc_wait(l, acc)
                wd = width_of(kind)
                out_ = ps[:, acc % 4, 0:wd]
                mms = []
                if job == "up":
                    for w1, w2 in PASSES:
                        for (kt, _), (_, wv) in zip(up_views(kind, w1), up_views(kind, w2)):
                            mms.append((latT[:, s % 2, w1, kt, :], wv))
                else:
                    for kt in range(KT):
                        for w1, w2 in PASSES:
                            mms.append((hT[:, w1, kt, s * P:(s + 1) * P], w_view(job, w2)[:, kt, :]))
                for n, (a, b) in enumerate(mms):
                    if s == 0 and job != "up" and n == len(mms) // 2:
                        pe.wait_ge(split_lo, l * NU + unit_of(job, 1) + 1 + 2)
                    last = pe.matmul(out_, a, b, start=(n == 0), stop=(n == len(mms) - 1))
                last.then_inc(acc_done, 1)

            for t in range(LEAD):
                norm_turn(-1, 3 * ST, t)
            pe.wait_ge(const_in, 16 * 3)
            with pe.Fori(0, DEPTH) as l:
                acc = turn = 0
                for e in EVENTS:
                    if e[0] == "acc":
                        kind, s = e[1], e[2]
                        if kind == "a":
                            pe.wait_ge(nt_free, l * TN + 2 * (s + 1) + 2)
                        if kind == "uq":
                            pe.wait_ge(turn_lo, l * len(TURNS) + TURNS.index(("turn", "lat", s)) + 1)
                        if kind == "a" and s == 2:
                            pe.wait_ge(down_free, l * 16 * NG + 4)
                        project(l, acc, kind, s)
                        if kind == "a" and s + LEAD < ST:
                            norm_turn(l, 0, s + LEAD)
                        acc += 1
                    elif e[0] == "turn":
                        kind, s = e[1], e[2]
                        if turn >= NTB:
                            pe.wait_ge(turn_lo, l * len(TURNS) + turn - NTB + 1)
                        if kind == "lat":
                            pe.wait_ge(lat_ready, l * ST + s + 1)
                            src = lat[:, s, :]
                        else:
                            se = ("acc", kind, s)
                            n = ACCS.index(se)
                            if kind in ACT_FREES:
                                pe.wait_ge(acc_free_act, l * ACT_FREE_N + frees_before(n + 1, True))
                            else:
                                pe.wait_ge(acc_free_dve, l * DVE_FREE_N + frees_before(n + 1, False))
                            src = stage[:, STAGED.index(se) % NSTG, :]
                        for j, wd in enumerate(TURN[kind][0]):
                            last = pe.transpose(ps[0:wd, 4 + turn % NTB, j * P:(j + 1) * P], src[:, j * P:j * P + wd],
                                                ident[:, :])
                        last.then_inc(turn_done, 1)
                        turn += 1

                pe.wait_ge(kr_in, (l + 1) * 16 * 4)

                def scores(i):
                    kind, h, q = ITEMS[i]
                    n = i // 8
                    hb = head[n % 2]
                    if i % 8 == 0:
                        done = sum(HEAD_DMAS[kd] for kd, _ in HEADS[n % 2:n + 1:2])
                        pe.wait_ge(head_in[n % 2], (l * HEAD_N[n % 2] + done) * 16)
                    if i >= 2:
                        pe.wait_ge(p_ready, l * NI + i - 1)
                    else:
                        pe.wait_ge(acc_free_dve, l * DVE_FREE_N + frees_before(job_end("cv") - 2 + 2 * i, False))
                    b0 = 2 * (i % 2)
                    if kind == "C":
                        cb, hf = q // 2, q % 2
                        grid = [hb[:, c * 1024:(c + 1) * 1024].rearrange("p (r c) -> p r c", c=GRID_W)
                                for c in range(3)]
                        qt = hb[:, 256 * cb + P * hf:256 * cb + P * (hf + 1)]
                        r0, c0 = key_row0(hf), c_cols(cb)
                        mm = [(qt, grid[1 + w][:, r0:r0 + CKR, c0:c0 + CKC]) for w in range(2)]
                        for k, (a, b) in enumerate(mm):
                            last = pe.matmul(ps[:, b0, 0:CW], a, b, start=(k == 0), stop=(k == 1))
                    else:
                        for kh in range(2):
                            cols = slice(kh * 512, kh * 512 + 512)
                            qt = hb[:, q * P:(q + 1) * P]
                            mm = [(qt, hb[:, 1024 * (1 + w):1024 * (2 + w)][:, cols]) for w in range(2)]
                            if kind == "A":
                                mm.append((hb[:, 3072 + q * P:3072 + (q + 1) * P], kR[:, cols]))
                            for k, (a, b) in enumerate(mm):
                                last = pe.matmul(ps[:, b0 + kh, :], a, b, start=(k == 0), stop=(k == len(mm) - 1))
                    last.then_inc(s_done, 1)

                def turns(i):
                    kind, h, q = ITEMS[i]
                    if i == 0:
                        pe.wait_ge(turn_lo, (l + 1) * len(TURNS))
                    if kind == "C":
                        pe.wait_ge(pn_ready, l * 8 * HC + i - 8 * (HA + HB) + 1)
                    else:
                        pe.wait_ge(p_ready, l * NI + i + 1)
                    for k, g in enumerate(ITEM_GROUPS[i]):
                        if g >= 2:
                            pe.wait_ge(t_lo, l * NGR + g - 1)
                        nk, _ = group_keys(g)
                        for j in range(nk):
                            c = (4 * k + j) * P
                            last = pe.transpose(ps[:, 4 + g % 2, j * P:(j + 1) * P], prob[:, i % 2, c:c + P],
                                                ident[:, :])
                        last.then_inc(t_done, 1)

                def weigh(b, part):
                    kind, h, q = ITEMS[4 * b]
                    hb = head[(b // 2) % 2]
                    bank = ps[:, 6 + b % 2, :]
                    if part == 0:
                        pe.wait_ge(t_lo, l * NGR + ITEM_GROUPS[4 * b + 3][-1] + 1)
                        n, k = b // 2, b // 2 % 2
                        done = sum(VALUE_DMAS[kd] for kd, _ in HEADS[k:n + 1:2])
                        pe.wait_ge(value_in[k], (l * VALUE_N[k] + done) * 16)
                        if b >= 2:
                            pe.wait_ge(o_ready, l * NMG + merges_before(b - 1))
                            pe.wait_ge(ot_ready, l * NB + b - 1)
                    if kind == "C":
                        c, w = part // 2, part % 2
                        cb = q // 2 + c
                        for n, (g, a, z) in enumerate(((1, 0, 256), (2, 0, 256), (0, 0, 128), (3, 128, 256))):
                            v = hb[:, 3072 + (4 * cb + g) * P:3072 + (4 * cb + g + 1) * P]
                            last = pe.matmul(bank[:, c * 256 + a:c * 256 + z], v,
                                             pT[:, b % 2, w, g, c * 256 + a:c * 256 + z],
                                             start=(w == 0 and n == 0), stop=(w == 1 and n == 3),
                                             skip_group_check=True)
                    else:
                        for kt in (2 * part, 2 * part + 1):
                            for w in range(2):
                                last = pe.matmul(bank, hb[:, 4096 + kt * P:4096 + (kt + 1) * P],
                                                 pT[:, b % 2, w, kt, :], start=(part == 0 and kt == 0 and w == 0),
                                                 stop=(part == 3 and kt == 7 and w == 1))
                    if part == 3:
                        last.then_inc(pv_done, 1)

                def merge(b):
                    kind, h, q = ITEMS[4 * b]
                    pe.wait_ge(ot_ready, l * NB + b + 1)
                    for k in range(8 if kind == "C" else 4):
                        c = k * P + (0 if kind == "C" else (b % 2) * 512)
                        last = pe.matmul(ps[:, 6 + b % 2, k * HD:(k + 1) * HD], oT[:, c:c + P], pair[:, :],
                                         start=True, stop=True)
                    last.then_inc(mg_done, 1)

                for i in range(NI + 12):
                    if i < NI:
                        scores(i)
                    if 2 <= i < NI + 2:
                        turns(i - 2)
                    if i >= 11 and (i - 11) % 4 == 0 and merged((i - 11) // 4):
                        merge((i - 11) // 4)
                    if i >= 6 and (i - 6) // 4 < NB:
                        weigh((i - 6) // 4, (i - 6) % 4)

                norm_turn(l, ST, 0)
                norm_turn(l, ST, 1)
                for s in range(ST):
                    pe.wait_ge(nt_free, l * TN + 2 * (ST + s + 1) + 2)
                    project(l, acc, "o0", s)
                    acc += 1
                    if s + 2 < ST:
                        norm_turn(l, ST, s + 2)
                for s in range(ST):
                    project(l, acc, "o1", s)
                    acc += 1
                    if s >= 2:
                        norm_turn(l, 2 * ST, s - 2)
                def up(g, unit, first):
                    pe.wait_ge(split_lo, l * NU + MLP0 + unit + 1 + 2)
                    for sh in range(2):
                        for ft in range(FT):
                            k = 2 * sh + ft
                            if first and k == 0:
                                pe.wait_ge(acc_free_dve, (l + 1) * DVE_FREE_N - 2)
                                pe.wait_ge(nt_free, l * TN + 2 * (2 * ST + ST // 2) + 2)
                            if first and k in (1, 2):
                                norm_turn(l, 2 * ST, ST - 3 + k)
                            if not first or k >= 2:
                                pe.wait_ge(relu_done, l * 4 * NG + 4 * g + k - 1)
                            if first and k == 2:
                                pe.wait_ge(nt_free, (l + 1) * TN + 2)
                            for kt in range(KT):
                                for w1, w2 in PASSES:
                                    last = pe.matmul(ps[:, k % 2, :], w_up[0 if first else 1][:, w1, kt, ft * P:(ft + 1) * P],
                                                     hT[:, w2, kt, sh * 512:(sh + 1) * 512],
                                                     start=(kt == 0 and (w1, w2) == PASSES[0]),
                                                     stop=(kt == KT - 1 and (w1, w2) == PASSES[-1]))
                            last.then_inc(up_tile, 1)

                def down(g, slot, unit, last_group=False):
                    pe.wait_ge(split_lo, l * NU + MLP0 + unit + 1 + 2)
                    pe.wait_ge(hid_ready, l * 4 * NG + 4 * g + 4 + 2)
                    for s in range(ST):
                        for nh in range(2):
                            m = 2 * s + nh
                            pe.wait_ge(down_free, l * 16 * NG + 16 * g + m + 1)
                            for ft in range(FT):
                                for w1, w2 in PASSES:
                                    last = pe.matmul(ps[:, 2 + m % 4, :], hid[slot][:, w1, ft, s * P:(s + 1) * P],
                                                     w_dn[1 if last_group else 0][:, w2, ft, nh * 512:(nh + 1) * 512],
                                                     start=(ft == 0 and (w1, w2) == PASSES[0]),
                                                     stop=(ft == FT - 1 and (w1, w2) == PASSES[-1]))
                            last.then_inc(down_tile, 1)
                        if last_group and s >= 2:
                            norm_turn(l, 3 * ST, s - 2)

                up(0, 0, True)
                with pe.Fori(0, NG // 2 - 1) as gg:
                    for k in range(2):
                        up(2 * gg + k + 1, 4 * gg + 2 * k + 1, False)
                        down(2 * gg + k, k, 4 * gg + 2 * k + 2)
                up(NG - 1, 2 * NG - 3, False)
                down(NG - 2, 0, 2 * NG - 2)
                down(NG - 1, 1, 2 * NG - 1, last_group=True)
            for t in range(LEAD, ST):
                norm_turn(DEPTH - 1, 3 * ST, t)


def stores_of(e):
    return 6 if e[1] == "cqk" else 2


def stores_before(k, n):
    return sum(stores_of(e) for e in STORED[k:n:NTS])


TST_N = [sum(stores_of(e) for e in STORED[k::NTS]) for k in range(NTS)]
TST_BEFORE = [stores_before(n % NTS, n) for n in range(len(STORED))]
HEAD_DMAS = {"A": 6 + 4, "B": 6, "C": 6}
VALUE_DMAS = {"A": 1, "B": 1, "C": 16}
HEAD_N = [sum(HEAD_DMAS[kd] for kd, _ in HEADS[k::2]) for k in range(2)]
VALUE_N = [sum(VALUE_DMAS[kd] for kd, _ in HEADS[k::2]) for k in range(2)]
MERGED = [ITEMS[4 * b][0] != "C" or b % 2 == 1 for b in range(NB)]
NMG = sum(MERGED)


def merged(b):
    return b < NB and MERGED[b]


def merges_before(b):
    return sum(MERGED[:b])


def turn_of(stg):
    e = STAGED[stg]
    return TURNS.index(("turn", e[1], e[2]))


def group_keys(g):
    it, half = GROUPS[g]
    kind, h, q = ITEMS[it]
    return (3, q % 2) if kind == "C" else (4, 4 * half)


def _pack_unit(w, n0):
    import numpy as np
    r, n = w.shape
    flat = np.ascontiguousarray(w.reshape(r // P, P, n).transpose(1, 0, 2)).reshape(P, -1)
    full = np.zeros((P, ULEN), np.float32)
    full[:, :flat.shape[1]] = flat
    return full


def _weight_stream(w_in, w_uq, w_ukv, w_out, w1, w2):
    import numpy as np
    ca, cb = CA, 3 * HB * HD
    b0, c0 = ca, ca + cb
    cols = {"a": (0, ca), "bq": (b0, b0 + 384), "bk": (b0 + 384, b0 + 768), "bv": (b0 + 768, b0 + 1152),
            "cqk": (c0, c0 + 512), "cv": (c0 + 512, c0 + 768)}
    out = np.zeros((DEPTH * NU + 2, P, ULEN), np.float32)
    for l in range(DEPTH):
        for job, (a, b) in cols.items():
            for hf in range(2):
                out[l * NU + 2 * JOBS.index(job) + hf] = _pack_unit(w_in[l, hf * 512:hf * 512 + 512, a:b], 0)
        uq = w_uq[l].reshape(QL, HA, HD + RA)
        uq = np.concatenate([uq[:, :, :HD].reshape(QL, -1), uq[:, :, HD:].reshape(QL, -1)], axis=1)
        ukv = w_ukv[l].reshape(KVL, HA, 2 * HD)
        ukv = np.concatenate([ukv[:, :, :HD].reshape(KVL, -1), ukv[:, :, HD:].reshape(KVL, -1)], axis=1)
        u = 2 * JOBS.index("up")
        out[l * NU + u] = _pack_unit(uq, 0)
        out[l * NU + u + 1] = _pack_unit(ukv, 0)
        for n in range(2):
            for hf in range(2):
                out[l * NU + 2 * JOBS.index(f"o{n}") + hf] = _pack_unit(
                    w_out[l, hf * 512:hf * 512 + 512, n * 512:n * 512 + 512], 0)
        for g in range(NG):
            out[l * NU + up_unit(g)] = _pack_unit(w1[l, :, g * FG:(g + 1) * FG], 0)
            out[l * NU + down_unit(g)] = _pack_unit(w2[l, g * FG:(g + 1) * FG, :], 0)
    return out


def _rotary():
    import numpy as np
    half = HD // 2
    inv = (np.float32(10000.0) ** (-np.arange(half, dtype=np.float32) / np.float32(half))).astype(np.float32)
    ang = np.arange(SEQ, dtype=np.float32)[:, None] * inv[None, :]
    shape = lambda a: np.ascontiguousarray(a.astype(np.float32).reshape(ST, P, half).transpose(1, 0, 2))
    return shape(np.cos(ang)), shape(np.sin(ang))


def _bias_b():
    import numpy as np
    d = np.arange(P)[:, None] + 896 - np.arange(1920)[None, :]
    n = ((abs(d) <= 64).astype(int) + ((d % 4 == 0) & (abs(d) <= 256)) + (d % 16 == 0))
    return np.where(n > 0, -np.log(np.maximum(n, 1)), -NEG).astype(np.float32)


def _bias_c(rpb):
    import numpy as np
    item = np.arange(8)
    cb, hf = item // 2, item % 2
    p, k = np.arange(P), np.arange(CW)
    rq = 8 * hf[:, None] + p[None, :] // 16
    cq = 16 * cb[:, None] + p[None, :] % 16
    rk = 4 * hf[:, None] + k[None, :] // CKC
    ck = np.array([c_cols(c) for c in cb])[:, None] + k[None, :] % CKC
    rs = np.clip(rq - 4, 0, ROWS - 8)[:, :, None]
    cs = np.clip(cq - 8, 0, GRID_W - 16)[:, :, None]
    rk, ck, rq, cq = rk[:, None, :], ck[:, None, :], rq[:, :, None], cq[:, :, None]
    ok = (rk >= rs) & (rk < rs + 8) & (ck >= cs) & (ck < cs + 16)
    dr = np.clip(rk - rq, -7, 7) + 7
    dc = np.clip(ck - cq, -15, 15) + 15
    full = np.where(ok[None, None], rpb[:, :, dr, dc], np.float32(NEG)).astype(np.float32)
    return np.ascontiguousarray(full.reshape(DEPTH, HC, 2, 4, P, CW).transpose(0, 1, 2, 4, 3, 5))


def kernel(**inputs):
    import numpy as np
    import concourse.bacc as bacc
    from concourse.bass_utils import run_bass_kernel_spmd

    a = {k: np.asarray(v) for k, v in inputs.items()}

    def wide(v):
        return np.ascontiguousarray(np.broadcast_to(v[..., None, :], v.shape[:-1] + (P, v.shape[-1])))

    cos, sin = _rotary()
    eye = np.eye(P, dtype=np.float32)
    out_gain = np.concatenate([a["out_norm_a"], a["out_norm_b"], a["out_norm_c"]], axis=-1)
    arrays = {
        "x": np.ascontiguousarray(a["x"][0]),
        "wstream": _weight_stream(a["w_in"], a["w_uq"], a["w_ukv"], a["w_out"], a["w_mlp_in"], a["w_mlp_out"]),
        "gains": wide(np.concatenate([np.stack([a["g_mix"], out_gain, a["g_mlp"]], axis=1).reshape(-1, DM),
                                      a["g_final"][None]])),
        "lat_gains": wide(np.concatenate([a["q_norm"], a["kv_norm"]], axis=-1)),
        "cos": cos, "sin": sin, "bias_b": _bias_b(), "bias_c": _bias_c(a["rpb"]),
        "ident": eye, "pair": np.concatenate([np.eye(HD, dtype=np.float32)] * 2, axis=0),
    }
    nc = bacc.Bacc("TRN2", target_bir_lowering=False, num_devices=1)
    arrays = {f"in_{k}": v for k, v in arrays.items()}
    args = [nc.dram_tensor(k, v.shape, mybir.dt.from_np(v.dtype), kind="ExternalInput").ap()
            for k, v in arrays.items()]
    out = nc.dram_tensor("out", (SEQ, DM), mybir.dt.float32, kind="ExternalOutput").ap()
    encoder(nc, *args, out)
    r = run_bass_kernel_spmd(nc, [arrays], core_ids=[0])
    return r.results[0]["out"].reshape(1, SEQ, DM)
```
